# Optimizing a Trainium2 kernel written in Bass

```python
import jax, jax.numpy as jnp
from jax import lax
import numpy as np

D_MODEL = 4096
BATCH = 1
SEQ = 256
DEPTH = 1

CHUNK = 64
PLE_DIM = 256
N_Q_HEADS = 32
N_KV_HEADS = 4
GROUP = N_Q_HEADS // N_KV_HEADS
HEAD_DIM = 64
D_ATTN = N_Q_HEADS * HEAD_DIM
D_KV = N_KV_HEADS * HEAD_DIM
WINDOW = 128
WINDOW_CHUNKS = WINDOW // CHUNK
D_CONV = D_MODEL // 2
CONV_WIDTH = 31
N_BRANCHES = 2
RMS_EPS = 1e-6
LN_EPS = 1e-5
D_IN = 3 * D_CONV + 2 * D_ATTN + 2 * D_KV

kernel_name = "hybrid_conformer_conv_swa_sink_block"

def rmsnorm(x, g):
    xf = x.astype(jnp.float32)
    y = xf * lax.rsqrt(jnp.mean(xf * xf, axis=-1, keepdims=True) + RMS_EPS)
    return (y * g.astype(jnp.float32)).astype(x.dtype)

def layernorm(x, g, b):
    xf = x.astype(jnp.float32)
    mu = jnp.mean(xf, axis=-1, keepdims=True)
    xc = xf - mu
    y = xc * lax.rsqrt(jnp.mean(xc * xc, axis=-1, keepdims=True) + LN_EPS)
    return (y * g.astype(jnp.float32) + b.astype(jnp.float32)).astype(x.dtype)

def split_in(z):
    widths = [D_CONV, D_CONV, D_CONV, D_ATTN, D_KV, D_KV]
    idx, acc = [], 0
    for w in widths:
        acc += w
        idx.append(acc)
    return jnp.split(z, idx, axis=-1)

def conv_branch(a, b, gate, w_dw, b_dw, ln_g, ln_b):
    u = a * jax.nn.sigmoid(b)
    u = jnp.pad(u, ((0, 0), (CONV_WIDTH - 1, 0), (0, 0)))
    y = lax.conv_general_dilated(
        u, w_dw[:, None, :].astype(u.dtype), window_strides=(1,), padding='VALID',
        dimension_numbers=('NWC', 'WIO', 'NWC'), feature_group_count=D_CONV)
    y = y + b_dw
    y = jax.nn.silu(layernorm(y, ln_g, ln_b))
    return y * jax.nn.silu(gate)

def swa_sink_attention(q, k, v, sinks):
    B, T, _ = q.shape
    nc = T // CHUNK
    qb = q.reshape(B, nc, CHUNK, N_KV_HEADS, GROUP, HEAD_DIM)

    def band(t):
        t = t.reshape(B, nc, CHUNK, N_KV_HEADS, HEAD_DIM)
        t = jnp.pad(t, ((0, 0), (WINDOW_CHUNKS - 1, 0), (0, 0), (0, 0), (0, 0)))
        return jnp.concatenate([t[:, j:j + nc] for j in range(WINDOW_CHUNKS)], axis=2)

    kb, vb = band(k), band(v)
    s = jnp.einsum('bcqhgd,bcshd->bchgqs', qb, kb).astype(jnp.float32) * (HEAD_DIM ** -0.5)
    key_chunk = (jnp.arange(nc)[:, None] - (WINDOW_CHUNKS - 1)
                 + jnp.arange(WINDOW)[None, :] // CHUNK)
    valid = key_chunk >= 0
    s = jnp.where(valid[None, :, None, None, None, :], s, -jnp.inf)
    sink = sinks.astype(jnp.float32).reshape(N_KV_HEADS, GROUP)[None, None, :, :, None, None]
    sink = jnp.broadcast_to(sink, s.shape[:-1] + (1,))
    pr = jax.nn.softmax(jnp.concatenate([s, sink], axis=-1), axis=-1)[..., :-1]
    o = jnp.einsum('bchgqs,bcshd->bcqhgd', pr.astype(vb.dtype), vb)
    return o.reshape(B, T, D_ATTN)

def setup_inputs(seed: int = 0) -> dict:
    key = jax.random.key(seed)
    ks = jax.random.split(key, 19)

    def nrm(k, shape, scale):
        return jax.random.normal(k, shape, jnp.float32) * scale

    return {
        "x": nrm(ks[0], (BATCH, SEQ, D_MODEL), 1.0),
        "p": nrm(ks[1], (DEPTH, BATCH, SEQ, PLE_DIM), 1.0),
        "w_in": nrm(ks[2], (DEPTH, D_MODEL, D_IN), D_MODEL ** -0.5),
        "b_in": nrm(ks[3], (DEPTH, D_IN), 0.02),
        "conv_w": nrm(ks[4], (DEPTH, CONV_WIDTH, D_CONV), CONV_WIDTH ** -0.5),
        "conv_b": nrm(ks[5], (DEPTH, D_CONV), 0.02),
        "conv_ln_g": 1.0 + nrm(ks[6], (DEPTH, D_CONV), 0.02),
        "conv_ln_b": nrm(ks[7], (DEPTH, D_CONV), 0.02),
        "attn_sinks": nrm(ks[8], (DEPTH, N_Q_HEADS), 1.0),
        "w_conv_out": nrm(ks[9], (DEPTH, D_CONV, D_MODEL), D_CONV ** -0.5),
        "w_attn_out": nrm(ks[10], (DEPTH, D_ATTN, D_MODEL), D_ATTN ** -0.5),
        "w_merge": nrm(ks[11], (DEPTH, D_MODEL, N_BRANCHES * D_MODEL), D_MODEL ** -0.5),
        "b_merge": nrm(ks[12], (DEPTH, N_BRANCHES * D_MODEL), 0.02),
        "w_out": nrm(ks[13], (DEPTH, D_MODEL, D_MODEL), D_MODEL ** -0.5),
        "pre_norm_g": 1.0 + nrm(ks[14], (DEPTH, D_MODEL), 0.02),
        "post_norm_g": 1.0 + nrm(ks[15], (DEPTH, D_MODEL), 0.02),
        "w_ple": nrm(ks[16], (DEPTH, PLE_DIM, D_MODEL), PLE_DIM ** -0.5),
        "w_ple_gate": nrm(ks[17], (DEPTH, D_MODEL, D_MODEL), D_MODEL ** -0.5),
        "ple_norm_g": 1.0 + nrm(ks[18], (DEPTH, D_MODEL), 0.02),
    }

def reference(x, p, w_in, b_in, conv_w, conv_b, conv_ln_g, conv_ln_b, attn_sinks,
              w_conv_out, w_attn_out, w_merge, b_merge, w_out, pre_norm_g, post_norm_g,
              w_ple, w_ple_gate, ple_norm_g):
    for i in range(DEPTH):
        h = rmsnorm(x, pre_norm_g[i])
        z = h @ w_in[i] + b_in[i]
        ca, cb, cg, q, k, v, ag = split_in(z)
        y_conv = conv_branch(ca, cb, cg, conv_w[i], conv_b[i],
                             conv_ln_g[i], conv_ln_b[i]) @ w_conv_out[i]
        y_attn = (swa_sink_attention(q, k, v, attn_sinks[i])
                  * jax.nn.silu(ag)) @ w_attn_out[i]
        g_conv, g_attn = jnp.split(jax.nn.sigmoid(h @ w_merge[i] + b_merge[i]), N_BRANCHES, axis=-1)
        y = (g_conv * y_conv + g_attn * y_attn) @ w_out[i]
        x = x + rmsnorm(y, post_norm_g[i])
        e = (p[i] @ w_ple[i]) * jax.nn.sigmoid(x @ w_ple_gate[i])
        x = x + rmsnorm(e, ple_norm_g[i])
    return x


_drawn_inputs = setup_inputs


def setup_inputs(seed=0):
    import zlib

    import numpy as np

    out = dict(_drawn_inputs(seed))
    spreads = {}
    factors = {'conv_ln_g': 15.259,
     'conv_ln_b': 15.903,
     'attn_sinks': 36.86,
     'b_merge': 8.0,
     'pre_norm_g': 2.871,
     'post_norm_g': 14.498,
     'ple_norm_g': 67.256,
     'b_in': 3.68,
     'conv_b': 6.01}
    for name, (base, spread) in spreads.items():
        noise = np.random.default_rng([zlib.crc32(name.encode()), seed]).standard_normal(out[name].shape)
        drawn = base * np.exp(spread * noise) if base else spread * noise
        out[name] = __import__('jax').numpy.asarray(drawn.astype(out[name].dtype))
    for name, factor in factors.items():
        out[name] = (out[name] * factor).astype(out[name].dtype)
    return out
```

```python
from contextlib import ExitStack

import numpy as np

import concourse.bass as bass
from concourse import mybir

F32 = mybir.dt.float32
F32R = mybir.dt.float32r
ALU = mybir.AluOpType
ACT = mybir.ActivationFunctionType
AX_X = mybir.AxisListType.X

P = 128
T = 256
D = 4096
DC = 2048
DKV = 256
PLE = 256
CHUNK = 64
NQ, NKV, HD = 32, 4, 64
TAPS = 31
RMS_EPS, LN_EPS = 1e-6, 1e-5

KT = D // P
KC = DC // P
CK = 4
GT = 2
GW = GT * P
RING = 4
AHEAD = RING - 1
ND = KT // CK
NC_ = KC // CK
GA = DC // GW
GD = D // GW
UOFF = 2

CA0, CB0, CG0, Q0 = 0, DC, 2 * DC, 3 * DC
K0 = 4 * DC
AG0 = K0 + 2 * DKV
V_BIN, V_BM = 0, 84
V_PRE = V_BM + 64
V_POST, V_PLEG = V_PRE + 32, V_PRE + 64
V_CB, V_LG, V_LB = V_PRE + 96, V_PRE + 112, V_PRE + 128
V_CW = V_PRE + 144
V_ALL = V_CW + 16 * TAPS

STAGES = [("kv", 2, 2 * ND), ("q", GA, GA * ND), ("ca", GA, GA * ND), ("cb", GA, GA * ND), ("ag", GA, GA * ND),
          ("attn", 2 * GD, GD * (ND + NC_)), ("cg", GA, GA * ND), ("conv", 2 * GD, GD * (ND + NC_)),
          ("out", GD, GD * ND), ("ple", GD, GD // 2), ("gate", GD, GD * ND)]
CHUNK0, GROUP0 = {}, {}
_c = _g = 0
for _name, _groups, _chunks in STAGES:
    CHUNK0[_name], GROUP0[_name] = _c, _g
    _c, _g = _c + _chunks, _g + _groups
CHUNKS, GROUPS = _c, _g
NCH = T // CHUNK
STEP = 3
SCORES, TURN, VALUES = 1, 4, 6
ROW_MAX, SCALED, TURNED, HEADS = 2, 3, 5, 7
SUM_LN = 1 + KC // 2 + 1
SUM_OUT = SUM_LN + KC // 2 + 1
SUM_E = SUM_OUT + GD + 1
NORM_STEPS = 6
Z0 = {"cb": 0, "ag": GA, "attn": 2 * GA, "cg": 2 * GA + GD, "conv": 3 * GA + GD, "gate": 3 * GA + 2 * GD}


def build(nc, xT, pT, vec, sinks, ident, ones, w_in, w_conv_out, w_attn_out, w_merge, w_out, w_ple, w_gate, outT):
    with ExitStack() as ctx:
        def sb(name, shape, dt, where=ctx):
            return where.enter_context(nc.sbuf_tensor(name, shape, dt))

        def sem(name):
            return ctx.enter_context(nc.semaphore(name))

        w_raw = sb("w_raw", [P, RING, CK, GW], F32)
        w_hi = sb("w_hi", [P, RING, CK, GW], F32R)
        w_lo = sb("w_lo", [P, RING, CK, GW], F32R)
        mov = sb("mov", [P, KT, 2, T], F32R)
        feat = sb("feat", [P, KT, T], F32)
        vecs = sb("vecs", [P, V_ALL], F32)
        ones_sb = sb("ones_sb", [P, P], F32)
        t_lo = sb("t_lo", [P, GT, T], F32)
        s_buf = sb("s_buf", [P, GT, T], F32)
        g_buf = sb("g_buf", [P, GT, T], F32)
        sums = sb("sums", [P, GT, T], F32)
        rstd = sb("rstd", [P, T], F32)
        with ExitStack() as u_ctx:
            x_blk = sb("x_blk", [P, 2, CK, T], F32, u_ctx)
            p_raw = sb("p_raw", [P, 2, T], F32, u_ctx)
            p_mov = sb("p_mov", [P, 2, 2, T], F32R, u_ctx)
        conv = sb("conv", [P, KC + UOFF, T], F32)
        with ExitStack() as z_ctx:
            x_in = sb("x_in", [P, KT, T], F32, z_ctx)
        with ExitStack() as z_ctx:
            kv_t = sb("kv_t", [P, 2 * GT, T], F32, z_ctx)
            k_dup = sb("k_dup", [P, NKV, T], F32, z_ctx)
            v_tok = sb("v_tok", [P, NCH, DKV], F32, z_ctx)
            q_st = sb("q_st", [P, NCH, 4, CHUNK], F32, z_ctx)
            k_st = sb("k_st", [P, T], F32, z_ctx)
            v_st = sb("v_st", [P, NCH, HD], F32, z_ctx)
            probs = sb("probs", [P, 4, P], F32, z_ctx)
            probs_t = sb("probs_t", [P, 4, P], F32, z_ctx)
            sink = sb("sink", [P, NKV, 4], F32, z_ctx)
            nsink = sb("nsink", [P, NKV, 4], F32, z_ctx)
            ident_sb = sb("ident_sb", [P, P], F32, z_ctx)
            negm = sb("negm", [P, 4], F32, z_ctx)
            smax = sb("smax", [P, 4], F32, z_ctx)
            rowsum = sb("rowsum", [P, 4], F32, z_ctx)
            sdiff = sb("sdiff", [P, 4], F32, z_ctx)
            esink = sb("esink", [P, 4], F32, z_ctx)
            denom = sb("denom", [P, 4], F32, z_ctx)
            rden = sb("rden", [P, 4], F32, z_ctx)
        with ExitStack() as z_ctx:
            branch = sb("branch", [P, KC, 2, T], F32R, z_ctx)
        e_ft = sb("e_ft", [P, KT, T], F32)

        def bank(name, shape):
            return ctx.enter_context(nc.psum_tensor(name, shape, F32))

        ps = bank("ps", [P, 4, 2 * T])
        ps_z = bank("ps_z", [P, GT, T])
        ps_sc = ps_z[:, :, :].rearrange("p a b -> p (a b)").rearrange("p (u k) -> p u k", u=4)
        ps_t = bank("ps_t", [P, 4, P])
        ps_o = bank("ps_o", [P, 4, 2 * CHUNK])
        ps_s = bank("ps_s", [P, 2 * T])

        ps_sc2 = ps_s[:, :].rearrange("p (u k) -> p u k", u=4)
        score = [ps_sc[:, 0], ps_sc[:, 1], ps_sc2[:, 0], ps_sc2[:, 1]]

        x_landed = [sem(f"x_landed{i}") for i in range(ND)]
        vec_landed, att_landed, kd_landed, p_landed = (sem(n) for n in ("vec_landed", "att_landed", "kd_landed", "p_landed"))
        xb_landed = [sem(f"xb_landed{i}") for i in range(2)]
        w_landed = [sem(f"w_landed{i}") for i in range(RING)]
        w_hi_ready, w_lo_ready, w_used = sem("w_hi_ready"), sem("w_lo_ready"), sem("w_used")
        lo_out, evacd = sem("lo_out"), sem("evacd")
        f_ready = sem("f_ready")
        ple_half = sem("ple_half")
        sq_ready, sq_used = sem("sq_ready"), sem("sq_used")
        h_ready, h_hi, mov_ready, y_hi = sem("h_ready"), sem("h_hi"), sem("mov_ready"), sem("y_hi")
        x1_part, x1_ready, x1_hi = sem("x1_part"), sem("x1_ready"), sem("x1_hi")
        p_hi, p_ready = sem("p_hi"), sem("p_ready")
        u_done = sem("u_done")
        b_ready, b_hi, b_done = sem("b_ready"), sem("b_hi"), sem("b_done")
        y_done = sem("y_done")
        conv_init, conv_tap = sem("conv_init"), sem("conv_tap")
        ln_mean, ln_cent, ln_ready, ln_act = sem("ln_mean"), sem("ln_cent"), sem("ln_ready"), sem("ln_act")
        sum_in, sum_added, stat_done = sem("sum_in"), sem("sum_added"), sem("stat_done")
        norm_step, root_ready = sem("norm_step"), sem("root_ready")
        e_ready, o_step, o_ready, o_stored = sem("e_ready"), sem("o_step"), sem("o_ready"), sem("o_stored")
        vt_done, vt_copied, staged = sem("vt_done"), sem("vt_copied"), sem("staged")
        sc_done, att_step, m_ready, p_exp, p_norm = (sem(n) for n in ("sc_done", "att_step", "m_ready", "p_exp", "p_norm"))
        t_done, pt_ready, pv_done, o_evacd = sem("t_done"), sem("pt_ready"), sem("pv_done"), sem("o_evacd")

        xT_v = xT.rearrange("(k p) t -> p k t", p=P)
        outT_v = outT.rearrange("(k p) t -> p k t", p=P)
        rows = {n: w.rearrange("(k p) n -> p k n", p=P) for n, w in
                (("in", w_in), ("merge", w_merge), ("attn", w_attn_out), ("conv", w_conv_out),
                 ("out", w_out), ("ple", w_ple), ("gate", w_gate))}

        block = ctx.enter_context(nc.Block())

        @block.sync
        def _(sp):
            def load_chunk(c, dyn, w, k0, col):
                if isinstance(dyn, int) and c + dyn < RING:
                    pass
                else:
                    sp.wait_ge(w_lo_ready, dyn + (c - RING + 1))
                sp.dma_start(w_raw[:, c % RING], rows[w][:, k0:k0 + CK, bass.ds(col, GW)]).then_inc(w_landed[c % RING], 16)

            def load_group(c, dyn, w, col, nk=ND):
                for i in range(nk):
                    load_chunk(c + i, dyn, w, CK * i, col)

            def load_stage(name, col0):
                with sp.Fori(0, GA // 2) as n:
                    for g in range(2):
                        load_group(CHUNK0[name] + g * ND, n * (2 * ND), "in", n * (2 * GW) + (col0 + g * GW))

            for b in range(ND):
                sp.dma_start(x_in[:, CK * b:CK * b + CK], xT_v[:, CK * b:CK * b + CK]).then_inc(x_landed[b], 16)
                if b == 0:
                    sp.dma_start(ones_sb[:], ones).then_inc(vec_landed, 16)
                    sp.dma_start(vecs[:], vec).then_inc(vec_landed, 16)
            for g in range(2):
                load_group(CHUNK0["kv"] + g * ND, 0, "in", K0 + g * GW)
            sp.wait_ge(evacd, 1)
            sp.dma_start(ident_sb[:], ident).then_inc(att_landed, 16)
            sp.dma_start(sink[:], sinks.rearrange("p (n u) -> p n u", u=4)).then_inc(att_landed, 16)
            for e in range(2):
                for half in range(2):
                    sp.dma_start(k_dup[HD * half:HD * half + HD, e:NKV:2, :],
                                 kv_t[HD * e:HD * e + HD, 0:GT, :]).then_inc(kd_landed, 16)
            load_stage("q", Q0)
            load_stage("ca", CA0)
            load_stage("cb", CB0)
            load_stage("ag", AG0)
            with sp.Fori(1, GD + 1) as j:
                c = CHUNK0["attn"] - (ND + NC_)
                load_group(c, j * (ND + NC_), "merge", j * GW + (D - GW))
                load_group(c + ND, j * (ND + NC_), "attn", j * GW - GW, NC_)
            load_stage("cg", CG0)
            with sp.Fori(0, GD) as j:
                load_group(CHUNK0["conv"], j * (ND + NC_), "merge", j * GW)
                load_group(CHUNK0["conv"] + ND, j * (ND + NC_), "conv", j * GW, NC_)
            sp.wait_ge(evacd, GROUP0["conv"])
            sp.dma_start(p_raw[:], pT.rearrange("(k p) t -> p k t", p=P)).then_inc(p_landed, 16)
            for b in range(2):
                sp.dma_start(x_blk[:, b], xT_v[:, CK * b:CK * b + CK]).then_inc(xb_landed[b], 16)
            with sp.Fori(0, GD) as j:
                load_group(CHUNK0["out"], j * ND, "out", j * GW)
            with sp.Fori(0, 2) as n:
                for i in range(RING):
                    c = CHUNK0["ple"] + i
                    sp.wait_ge(w_lo_ready, n * RING + (c - RING + 1))
                    sp.dma_start(w_raw[:, c % RING].rearrange("p a b -> p (a b)").rearrange("p (k n) -> p k n", k=2),
                                 rows["ple"][:, :, bass.ds(n * (RING * 2 * GW) + i * 2 * GW, 2 * GW)]
                                 ).then_inc(w_landed[c % RING], 16)
            with sp.Fori(0, GD) as j:
                load_group(CHUNK0["gate"], j * ND, "gate", j * GW)
            for b in range(ND):
                sp.wait_ge(o_ready, b + 1)
                sp.dma_start(outT_v[:, CK * b:CK * b + CK], e_ft[:, CK * b:CK * b + CK]).then_inc(o_stored, 16)
            sp.wait_ge(o_stored, 16 * ND)

        @block.gpsimd
        def _(pool):
            def clear(done):
                pool.wait_ge(stat_done, done)
                nc.gpsimd.memset(sums[:], 0.0).then_inc(sum_added, 1)

            def add(src, n):
                pool.wait_ge(sum_added, n)
                nc.gpsimd.tensor_tensor(sums[:], sums[:], src, ALU.add).then_inc(sum_added, 1)

            nc.gpsimd.memset(sums[:], 0.0).then_inc(sum_added, 1)
            with pool.Fori(0, KC // 2) as i:
                pool.wait_ge(conv_tap, i * (2 * (TAPS - 1)) + 2 * (TAPS - 1))
                add(conv[:, bass.ds(i * 2, 2)], i + 1)
            clear(2)
            for i in range(KC // 2):
                pool.wait_ge(sum_in, i + 1)
                add((s_buf, g_buf)[i % 2][:], SUM_LN + i)
            clear(3)
            with pool.Fori(0, GD) as j:
                pool.wait_ge(sum_in, j + (KC // 2 + 1))
                add(s_buf[:], j + SUM_OUT)
            clear(4)
            with pool.Fori(0, GD) as j:
                pool.wait_ge(sum_in, j + (KC // 2 + GD + 1))
                add(s_buf[:], j + SUM_E)

        @block.scalar
        def _(act):
            def split(c, dyn=0):
                act.wait_ge(w_landed[c % RING], dyn * 16 // RING + 16 * (c // RING + 1) if isinstance(dyn, int)
                            else dyn * (16 // RING) + 16 * (c // RING + 1))
                if c >= RING or not isinstance(dyn, int):
                    act.wait_ge(w_used, dyn + (c - RING + 1))
                nc.scalar.copy(w_hi[:, c % RING], w_raw[:, c % RING]).then_inc(w_hi_ready, 1)

            def splits(c, dyn=0, nk=ND, hook=None, stop=CHUNKS):
                for i in range(nk):
                    if c + i + AHEAD < stop:
                        split(c + i + AHEAD, dyn)
                    if hook:
                        hook(i)

            def half_out(g, gdyn, c_end, cdyn):
                act.wait_ge(w_used, cdyn + c_end)
                if g > 0 or not isinstance(gdyn, int):
                    act.wait_ge(evacd, gdyn + g)
                nc.scalar.copy(t_lo[:], ps[:, 2 * (g % 2):2 * (g % 2) + 2, T:]).then_inc(lo_out, 1)

            def function(g, gdyn, dst, f):
                act.wait_ge(evacd, gdyn + (g + 1))
                nc.scalar.activation(dst, ps_z[:], f).then_inc(f_ready, 1)

            bufs = (s_buf, g_buf, t_lo)
            for b in range(KT // 2):
                act.wait_ge(x_landed[b // 2], 16)
                if b >= 3:
                    act.wait_ge(sq_used, b - 2)
                nc.scalar.activation(bufs[b % 3][:], x_in[:, 2 * b:2 * b + 2], ACT.Square).then_inc(sq_ready, 1)
            for c in range(AHEAD):
                split(c)
            act.wait_ge(norm_step, 2)
            nc.scalar.activation(rstd[:], rstd[:], ACT.Sqrt).then_inc(root_ready, 1)

            def h_high(i):
                act.wait_ge(h_ready, i + 1)
                nc.scalar.copy(mov[:, CK * i:CK * i + CK, 0], x_in[:, CK * i:CK * i + CK]).then_inc(h_hi, 1)

            for g in range(2):
                splits(g * ND, hook=h_high if g == 0 else None)
                half_out(g, 0, (g + 1) * ND, 0)

            with act.Fori(0, GA // 2) as n:
                for g in range(2):
                    splits(CHUNK0["q"] + g * ND, n * (2 * ND))
                    half_out(GROUP0["q"] + g, n * 2, CHUNK0["q"] + (g + 1) * ND, n * (2 * ND))

            with act.Fori(0, NKV) as n:
                def attention(pos):
                    for c in range(NCH):
                        nk = P if c else CHUNK
                        if pos == ROW_MAX + STEP * c:
                            act.wait_ge(m_ready, n * NCH + (c + 1))
                            for u in range(4):
                                nc.scalar.activation(probs[:, u, 0:nk], score[u][:, 0:nk], ACT.Exp, bias=negm[:, u:u + 1],
                                                     scale=HD ** -0.5, accum_out=rowsum[:, u:u + 1])
                            nc.scalar.activation(esink[:], sdiff[:], ACT.Exp).then_inc(p_exp, 1)
                        if pos == TURNED + STEP * c:
                            act.wait_ge(t_done, n * NCH + (c + 1))
                            nc.scalar.copy(probs_t[0:nk], ps_t[0:nk]).then_inc(pt_ready, 1)

                for g in range(2):
                    splits(CHUNK0["ca"] + g * ND, n * (2 * ND), hook=lambda i: attention(g * ND + i))
                    half_out(GROUP0["ca"] + g, n * 2, CHUNK0["ca"] + (g + 1) * ND, n * (2 * ND))

            with act.Fori(0, GA // 2) as n:
                for g in range(2):
                    splits(CHUNK0["cb"] + g * ND, n * (2 * ND))
                    half_out(GROUP0["cb"] + g, n * 2, CHUNK0["cb"] + (g + 1) * ND, n * (2 * ND))
                    function(GROUP0["cb"] + g, n * 2, s_buf[:], ACT.Sigmoid)

            with act.Fori(0, GA // 2) as n:
                for g in range(2):
                    splits(CHUNK0["ag"] + g * ND, n * (2 * ND))
                    half_out(GROUP0["ag"] + g, n * 2, CHUNK0["ag"] + (g + 1) * ND, n * (2 * ND))
                    function(GROUP0["ag"] + g, n * 2, s_buf[:], ACT.Silu)
                    act.wait_ge(b_ready, n * 2 + (g + 1))
                    nc.scalar.copy(branch[:, bass.ds(n * (2 * GT) + g * GT, GT), 0], feat[:, bass.ds(n * (2 * GT) + g * GT, GT)]
                                   ).then_inc(b_hi, 1)

            with act.Fori(0, GD // 2) as i:
                act.wait_ge(u_done, GA)
                act.wait_ge(sum_added, i + 1)
                for a in range(2):
                    nc.scalar.activation(conv[:, bass.ds(i * 2 + a, 1)], conv[:, bass.ds(i * 2 + (a + UOFF), 1)], ACT.Identity,
                                         bias=vecs[:, bass.ds(i * 2 + (V_CB + a), 1)],
                                         scale=vecs[:, bass.ds(i * (2 * TAPS) + (V_CW + a * TAPS + TAPS - 1), 1)]
                                         ).then_inc(conv_init, 1)
                for jj in range(2):
                    c, g = CHUNK0["attn"] + jj * (ND + NC_), GROUP0["attn"] + 2 * jj
                    cd, gd = i * (2 * (ND + NC_)), i * 4
                    splits(c, cd)
                    half_out(g, gd, c + ND, cd)
                    function(g, gd, g_buf[:], ACT.Sigmoid)
                    splits(c + ND, cd, NC_)
                    half_out(g + 1, gd, c + ND + NC_, cd)

            def conv_gate(n, g):
                tile = n * (2 * GT) + g * GT
                act.wait_ge(ln_ready, n * 2 + (g + 1))
                for a in range(GT):
                    nc.scalar.activation(g_buf[:, a], s_buf[:, a], ACT.Silu, bias=vecs[:, bass.ds(tile + (V_LB + a), 1)],
                                         scale=vecs[:, bass.ds(tile + (V_LG + a), 1)]).then_inc(ln_act, 1)
                half_out(GROUP0["cg"] + g, n * 2, CHUNK0["cg"] + (g + 1) * ND, n * (2 * ND))
                function(GROUP0["cg"] + g, n * 2, s_buf[:], ACT.Silu)
                act.wait_ge(b_ready, n * 2 + (GA + g + 1))
                nc.scalar.copy(branch[:, bass.ds(tile, GT), 0], g_buf[:]).then_inc(b_hi, 1)

            def ln_squares(i):
                if i < KC // 2:
                    act.wait_ge(ln_cent, i + 1)
                    if i >= 2:
                        act.wait_ge(sum_added, SUM_LN + i - 1)
                    nc.scalar.activation((s_buf, g_buf)[i % 2][:], conv[:, 2 * i:2 * i + 2], ACT.Square).then_inc(sum_in, 1)

            splits(CHUNK0["cg"], hook=ln_squares)
            act.wait_ge(norm_step, NORM_STEPS + 2)
            nc.scalar.activation(rstd[:], rstd[:], ACT.Sqrt).then_inc(root_ready, 1)
            conv_gate(0, 0)
            splits(CHUNK0["cg"] + ND)
            conv_gate(0, 1)
            with act.Fori(1, GA // 2) as n:
                for g in range(2):
                    splits(CHUNK0["cg"] + g * ND, n * (2 * ND))
                    conv_gate(n, g)

            with act.Fori(0, GD) as j:
                c, g = CHUNK0["conv"], GROUP0["conv"]
                splits(c, j * (ND + NC_))
                half_out(g, j * 2, c + ND, j * (ND + NC_))
                function(g, j * 2, g_buf[:], ACT.Sigmoid)
                splits(c + ND, j * (ND + NC_), NC_)
                half_out(g + 1, j * 2, c + ND + NC_, j * (ND + NC_))

            def y_high(i):
                act.wait_ge(y_done, GD + GD * 2)
                nc.scalar.copy(mov[:, CK * i:CK * i + CK, 0], feat[:, CK * i:CK * i + CK]).then_inc(y_hi, 1)

            def out_group(g, j):
                half_out(GROUP0["out"] + g, j, CHUNK0["out"] + (g + 1) * ND, j * ND)
                act.wait_ge(evacd, j + (GROUP0["out"] + g + 1))
                act.wait_ge(sum_added, j + (SUM_OUT + g))
                nc.scalar.activation(s_buf[:], feat[:, bass.ds(j * GT + g * GT, GT)], ACT.Square).then_inc(sum_in, 1)

            splits(CHUNK0["out"], hook=y_high)
            out_group(0, 0)
            splits(CHUNK0["out"] + ND)
            out_group(1, 0)
            with act.Fori(1, GD // 2) as n:
                for g in range(2):
                    splits(CHUNK0["out"] + g * ND, n * (2 * ND))
                    out_group(g, n * 2)

            act.wait_ge(p_landed, 16)
            nc.scalar.copy(p_mov[:, :, 0], p_raw[:]).then_inc(p_hi, 1)
            act.wait_ge(norm_step, 2 * NORM_STEPS + 2)
            nc.scalar.activation(rstd[:], rstd[:], ACT.Sqrt).then_inc(root_ready, 1)
            for i in range(GD // 2):
                split(CHUNK0["ple"] + i + AHEAD)
                g = GROUP0["ple"] + 2 * i
                act.wait_ge(ple_half, i + 1)
                act.wait_ge(evacd, g)
                nc.scalar.copy(t_lo[:], ps[:, 0:2, T:]).then_inc(lo_out, 1)
                half_out(g + 1, 0, CHUNK0["ple"] + i + 1, 0)
                act.wait_ge(x1_ready, i + 1)
                nc.scalar.copy(mov[:, CK * i:CK * i + CK, 0], feat[:, CK * i:CK * i + CK]).then_inc(x1_hi, 1)
                if i + 2 < ND:
                    act.dma_start(x_blk[:, i % 2], xT_v[:, CK * (i + 2):CK * (i + 3)]).then_inc(xb_landed[i % 2], 16)

            def gate_group(g, j):
                half_out(GROUP0["gate"] + g, j, CHUNK0["gate"] + (g + 1) * ND, j * ND)
                act.wait_ge(sum_added, j + (SUM_E + g))
                function(GROUP0["gate"] + g, j, s_buf[:], ACT.Sigmoid)
                act.wait_ge(e_ready, j + (g + 1))
                nc.scalar.activation(s_buf[:], e_ft[:, bass.ds(j * GT + g * GT, GT)], ACT.Square).then_inc(sum_in, 1)

            with act.Fori(0, GD // 2 - 1) as n:
                for g in range(2):
                    splits(CHUNK0["gate"] + g * ND, n * (2 * ND))
                    gate_group(g, n * 2)
            for g in range(GD - 2, GD):
                splits(CHUNK0["gate"] + g * ND)
                gate_group(g, 0)
            act.wait_ge(norm_step, 3 * NORM_STEPS + 2)
            nc.scalar.activation(rstd[:], rstd[:], ACT.Sqrt).then_inc(root_ready, 1)

        @block.vector
        def _(dve):
            def split(c, dyn=0):
                dve.wait_ge(w_hi_ready, dyn + (c + 1))
                nc.vector.tensor_tensor(w_lo[:, c % RING], w_raw[:, c % RING], w_hi[:, c % RING].bitcast(F32),
                                        ALU.subtract).then_inc(w_lo_ready, 1)

            def splits(c, dyn=0, nk=ND, hook=None, stop=CHUNKS):
                for i in range(nk):
                    if c + i + AHEAD < stop:
                        split(c + i + AHEAD, dyn)
                    if hook:
                        hook(i)

            def whole_out(g, gdyn, dst, bias=None):
                dve.wait_ge(lo_out, gdyn + (g + 1))
                s = 2 * (g % 2)
                if bias is None:
                    nc.vector.tensor_tensor(dst, ps[:, s:s + 2, 0:T], t_lo[:], ALU.add).then_inc(evacd, 1)
                    return
                for a in range(GT):
                    last = nc.vector.scalar_tensor_tensor(out=dst(a), in0=ps[:, s + a, 0:T], scalar=vecs[:, bass.ds(bias + a, 1)],
                                                          in1=t_lo[:, a], op0=ALU.add, op1=ALU.add)
                last.then_inc(evacd, 1)

            def norm(k, n, eps):
                v, w = g_buf[:, 0], g_buf[:, 1]
                s = k * NORM_STEPS
                nc.vector.tensor_scalar(v, ps_s[:, 0:T], 1.0 / n, eps, ALU.mult, ALU.add).then_inc(norm_step, 1)
                dve.wait_ge(norm_step, s + 1)
                nc.vector.reciprocal(rstd[:], v).then_inc(norm_step, 1)
                dve.wait_ge(root_ready, k + 1)
                nc.vector.tensor_tensor(w, rstd[:], rstd[:], ALU.mult).then_inc(norm_step, 1)
                dve.wait_ge(norm_step, s + 3)
                nc.vector.tensor_tensor(w, w, v, ALU.mult).then_inc(norm_step, 1)
                dve.wait_ge(norm_step, s + 4)
                nc.vector.tensor_scalar(w, w, -0.5, 1.5, ALU.mult, ALU.add).then_inc(norm_step, 1)
                dve.wait_ge(norm_step, s + 5)
                nc.vector.tensor_tensor(rstd[:], rstd[:], w, ALU.mult).then_inc(norm_step, 1)
                dve.wait_ge(norm_step, s + 6)

            def low(dst, whole, high):
                return nc.vector.tensor_tensor(dst, whole, high.bitcast(F32), ALU.subtract)

            for c in range(AHEAD):
                split(c)
            dve.wait_ge(stat_done, 1)
            dve.wait_ge(vec_landed, 32)
            norm(0, D, RMS_EPS)

            def h_block(k):
                for t in range(CK * k, CK * k + CK):
                    last = nc.vector.scalar_tensor_tensor(out=x_in[:, t], in0=x_in[:, t], scalar=vecs[:, V_PRE + t:V_PRE + t + 1],
                                                          in1=rstd[:], op0=ALU.mult, op1=ALU.mult)
                last.then_inc(h_ready, 1)

            def h_low(i):
                if i + 1 < ND:
                    h_block(i + 1)
                dve.wait_ge(h_hi, i + 1)
                r = slice(CK * i, CK * i + CK)
                low(mov[:, r, 1], x_in[:, r], mov[:, r, 0]).then_inc(mov_ready, 1)

            h_block(0)
            for g in range(2):
                splits(g * ND, hook=h_low if g == 0 else None)
                whole_out(g, 0, lambda a: kv_t[:, GT * g + a], V_BIN + K0 // P + GT * g)

            with dve.Fori(0, GA // 2) as n:
                for g in range(2):
                    splits(CHUNK0["q"] + g * ND, n * (2 * ND))
                    tile = n * (2 * GT) + g * GT
                    whole_out(GROUP0["q"] + g, n * 2, lambda a: feat[:, bass.ds(tile + a, 1)], tile + (V_BIN + Q0 // P))

            dve.wait_ge(vt_done, 1)
            for a, src in enumerate((ps_t, ps_sc)):
                nc.vector.tensor_copy(v_tok[0:CHUNK, 0, a * P:a * P + P], src[0:CHUNK, 0])
                nc.vector.tensor_copy(v_tok[:, 1:NCH, a * P:a * P + P], src[:, 1:NCH]).then_inc(vt_copied, 1)
            dve.wait_ge(att_landed, 32)
            nc.vector.tensor_scalar(nsink[:], sink[:], -1.0, None, ALU.mult).then_inc(vt_copied, 1)
            nc.vector.memset(probs[:], 0.0).then_inc(o_evacd, 1)
            dve.wait_ge(vt_copied, 3)
            dve.wait_ge(kd_landed, 64)
            dve.wait_ge(evacd, GROUP0["ca"])

            with dve.Fori(0, NKV) as n:
                nc.vector.tensor_copy(q_st[:].rearrange("p c a t -> p a c t"),
                                      feat[:, bass.ds(n * 4, 4)].rearrange("p a (c t) -> p a c t", t=CHUNK))
                nc.vector.tensor_copy(k_st[:], k_dup[:, bass.ds(n, 1)])
                nc.vector.tensor_copy(v_st[0:CHUNK, 0:1], v_tok[0:CHUNK, 0:1, bass.ds(n * HD, HD)])
                nc.vector.tensor_copy(v_st[:, 1:NCH], v_tok[:, 1:NCH, bass.ds(n * HD, HD)]).then_inc(staged, 1)

                def head_out(c):
                    dve.wait_ge(pv_done, n * NCH + (c + 1))
                    nc.vector.tensor_scalar(feat[:, bass.ds(n * 4, 4), c * CHUNK:(c + 1) * CHUNK], ps_o[:, :, 0:CHUNK], 1.0, None,
                                            ALU.mult).then_inc(o_evacd, 1)

                def attention(pos):
                    for c in range(NCH):
                        nk = P if c else CHUNK
                        s, st = n * (4 * NCH), 4 * c
                        if pos == ROW_MAX + STEP * c:
                            dve.wait_ge(sc_done, n * NCH + (c + 1))
                            nc.vector.tensor_reduce(smax[:, 0:2], ps_sc[:, 0:2, 0:nk], AX_X, ALU.max)
                            nc.vector.tensor_reduce(smax[:, 2:4], ps_sc2[:, 0:2, 0:nk], AX_X, ALU.max).then_inc(att_step, 1)
                            dve.wait_ge(att_step, s + (st + 1))
                            nc.vector.scalar_tensor_tensor(out=negm[:], in0=smax[:], scalar=-(HD ** -0.5), in1=nsink[:, bass.ds(n, 1)],
                                                           op0=ALU.mult, op1=ALU.min).then_inc(att_step, 1)
                            dve.wait_ge(att_step, s + (st + 2))
                            nc.vector.tensor_tensor(sdiff[:], sink[:, bass.ds(n, 1)], negm[:], ALU.add).then_inc(m_ready, 1)
                        if pos == SCALED + STEP * c:
                            dve.wait_ge(p_exp, n * NCH + (c + 1))
                            nc.vector.tensor_tensor(denom[:], rowsum[:], esink[:], ALU.add).then_inc(att_step, 1)
                            dve.wait_ge(att_step, s + (st + 3))
                            nc.vector.reciprocal(rden[:], denom[:]).then_inc(att_step, 1)
                            dve.wait_ge(att_step, s + (st + 4))
                            for u in range(4):
                                last = nc.vector.tensor_scalar(probs[:, u, 0:nk], probs[:, u, 0:nk], rden[:, u:u + 1], None, ALU.mult)
                            last.then_inc(p_norm, 1)
                        if pos == HEADS + STEP * c:
                            head_out(c)

                for g in range(2):
                    splits(CHUNK0["ca"] + g * ND, n * (2 * ND), hook=lambda i: attention(g * ND + i))
                    tile = n * (2 * GT) + g * GT
                    whole_out(GROUP0["ca"] + g, n * 2, lambda a: conv[:, bass.ds(tile + (UOFF + a), 1)], tile + (V_BIN + CA0 // P))
                head_out(NCH - 1)
                dve.wait_ge(o_evacd, n * NCH + (NCH + 1))

            with dve.Fori(0, GA // 2) as n:
                for g in range(2):
                    splits(CHUNK0["cb"] + g * ND, n * (2 * ND))
                    tile = n * (2 * GT) + g * GT
                    whole_out(GROUP0["cb"] + g, n * 2, lambda a: ps_z[:, a], tile + (V_BIN + CB0 // P))
                    dve.wait_ge(f_ready, n * 2 + (Z0["cb"] + g + 1))
                    u = conv[:, bass.ds(tile + UOFF, GT)]
                    nc.vector.tensor_tensor(u, u, s_buf[:], ALU.mult).then_inc(u_done, 1)

            with dve.Fori(0, GA // 2) as n:
                for g in range(2):
                    splits(CHUNK0["ag"] + g * ND, n * (2 * ND))
                    tile = n * (2 * GT) + g * GT
                    whole_out(GROUP0["ag"] + g, n * 2, lambda a: ps_z[:, a], tile + (V_BIN + AG0 // P))
                    dve.wait_ge(f_ready, n * 2 + (Z0["ag"] + g + 1))
                    o = feat[:, bass.ds(tile, GT)]
                    nc.vector.tensor_tensor(o, o, s_buf[:], ALU.mult).then_inc(b_ready, 1)
                    dve.wait_ge(b_hi, n * 2 + (g + 1))
                    low(branch[:, bass.ds(tile, GT), 1], o, branch[:, bass.ds(tile, GT), 0]).then_inc(b_done, 1)

            with dve.Fori(0, GD // 2) as i:
                taps = [(1 + j * (2 * (ND + NC_) - 1) // (TAPS - 1), j) for j in range(TAPS - 1)]

                def conv_taps(pos):
                    for at, j in taps:
                        if at != pos:
                            continue
                        lag = TAPS - 1 - j
                        for a in range(2):
                            if j == 0:
                                dve.wait_ge(conv_init, i * 2 + (a + 1))
                            else:
                                dve.wait_ge(conv_tap, i * (2 * (TAPS - 1)) + (2 * j + a - 1))
                            y = conv[:, bass.ds(i * 2 + a, 1), lag:T]
                            nc.vector.scalar_tensor_tensor(out=y, in0=conv[:, bass.ds(i * 2 + (a + UOFF), 1), 0:T - lag],
                                                           scalar=vecs[:, bass.ds(i * (2 * TAPS) + (V_CW + a * TAPS + j), 1)],
                                                           in1=y, op0=ALU.mult, op1=ALU.add).then_inc(conv_tap, 1)

                for jj in range(2):
                    base = jj * (ND + NC_)
                    c, g = CHUNK0["attn"] + base, GROUP0["attn"] + 2 * jj
                    cd, gd = i * (2 * (ND + NC_)), i * 4
                    splits(c, cd, hook=lambda k: conv_taps(base + k))
                    whole_out(g, gd, lambda a: ps_z[:, a], i * (2 * GT) + (V_BM + KT + jj * GT))
                    splits(c + ND, cd, NC_, hook=lambda k: conv_taps(base + ND + k))
                    whole_out(g + 1, gd, s_buf[:])
                    dve.wait_ge(f_ready, i * 2 + (Z0["attn"] + jj + 1))
                    dve.wait_ge(evacd, gd + (g + 2))
                    nc.vector.tensor_tensor(feat[:, bass.ds(i * (2 * GT) + jj * GT, GT)], s_buf[:], g_buf[:], ALU.mult).then_inc(y_done, 1)

            def conv_gate(n, g):
                tile = n * (2 * GT) + g * GT
                for a in range(GT):
                    last = nc.vector.tensor_tensor(s_buf[:, a:a + 1], conv[:, bass.ds(tile + a, 1)], rstd[:], ALU.mult)
                last.then_inc(ln_ready, 1)
                whole_out(GROUP0["cg"] + g, n * 2, lambda a: ps_z[:, a], tile + (V_BIN + CG0 // P))
                dve.wait_ge(ln_act, n * 4 + (2 * g + 2))
                dve.wait_ge(f_ready, n * 2 + (Z0["cg"] + g + 1))
                nc.vector.tensor_tensor(g_buf[:], g_buf[:], s_buf[:], ALU.mult).then_inc(b_ready, 1)
                dve.wait_ge(b_hi, n * 2 + (GA + g + 1))
                low(branch[:, bass.ds(tile, GT), 1], g_buf[:], branch[:, bass.ds(tile, GT), 0]).then_inc(b_done, 1)

            def centre(i):
                if i == 0:
                    dve.wait_ge(stat_done, 2)
                    nc.vector.tensor_scalar(rstd[:], ps_s[:, 0:T], 1.0 / DC, None, ALU.mult).then_inc(ln_mean, 1)
                    dve.wait_ge(ln_mean, 1)
                for b in ((0, 1), (2, 3), (4, 5), (6, 7)).__getitem__(i) if i < 4 else ():
                    for a in range(2):
                        y = conv[:, 2 * b + a]
                        last = nc.vector.tensor_tensor(y, y, rstd[:], ALU.subtract)
                    last.then_inc(ln_cent, 1)

            splits(CHUNK0["cg"], hook=centre)
            dve.wait_ge(ln_cent, KC // 2)
            dve.wait_ge(stat_done, 3)
            norm(1, DC, LN_EPS)
            conv_gate(0, 0)
            splits(CHUNK0["cg"] + ND)
            conv_gate(0, 1)
            with dve.Fori(1, GA // 2) as n:
                for g in range(2):
                    splits(CHUNK0["cg"] + g * ND, n * (2 * ND))
                    conv_gate(n, g)

            with dve.Fori(0, GD) as j:
                c, g, gd = CHUNK0["conv"], GROUP0["conv"], j * 2
                splits(c, j * (ND + NC_))
                whole_out(g, gd, lambda a: ps_z[:, a], j * GT + V_BM)
                splits(c + ND, j * (ND + NC_), NC_)
                whole_out(g + 1, gd, s_buf[:])
                dve.wait_ge(f_ready, j + (Z0["conv"] + 1))
                dve.wait_ge(evacd, gd + (g + 2))
                nc.vector.tensor_tensor(s_buf[:], s_buf[:], g_buf[:], ALU.mult).then_inc(y_done, 1)
                dve.wait_ge(y_done, j * 2 + (GD + 1))
                y = feat[:, bass.ds(j * GT, GT)]
                nc.vector.tensor_tensor(y, y, s_buf[:], ALU.add).then_inc(y_done, 1)

            def y_low(i):
                dve.wait_ge(y_hi, i + 1)
                r = slice(CK * i, CK * i + CK)
                low(mov[:, r, 1], feat[:, r], mov[:, r, 0]).then_inc(mov_ready, 1)

            splits(CHUNK0["out"], hook=y_low)
            whole_out(GROUP0["out"], 0, feat[:, 0:GT])
            splits(CHUNK0["out"] + ND)
            whole_out(GROUP0["out"] + 1, 0, feat[:, GT:2 * GT])
            with dve.Fori(1, GD // 2) as n:
                for g in range(2):
                    splits(CHUNK0["out"] + g * ND, n * (2 * ND))
                    whole_out(GROUP0["out"] + g, n * 2, feat[:, bass.ds(n * (2 * GT) + g * GT, GT)])

            dve.wait_ge(p_hi, 1)
            low(p_mov[:, :, 1], p_raw[:], p_mov[:, :, 0]).then_inc(p_ready, 1)
            dve.wait_ge(stat_done, 4)
            norm(2, D, RMS_EPS)
            for i in range(GD // 2):
                split(CHUNK0["ple"] + i + AHEAD)
                for a in range(2):
                    whole_out(GROUP0["ple"] + 2 * i + a, 0, e_ft[:, CK * i + GT * a:CK * i + GT * a + GT])
                r = slice(CK * i, CK * i + CK)
                for t in range(CK * i, CK * i + CK):
                    last = nc.vector.scalar_tensor_tensor(out=feat[:, t], in0=feat[:, t], scalar=vecs[:, V_POST + t:V_POST + t + 1],
                                                          in1=rstd[:], op0=ALU.mult, op1=ALU.mult)
                last.then_inc(x1_part, 1)
                dve.wait_ge(x1_part, i + 1)
                dve.wait_ge(xb_landed[i % 2], 16 * (i // 2 + 1))
                nc.vector.tensor_tensor(feat[:, r], feat[:, r], x_blk[:, i % 2], ALU.add).then_inc(x1_ready, 1)
                dve.wait_ge(x1_hi, i + 1)
                low(mov[:, r, 1], feat[:, r], mov[:, r, 0]).then_inc(mov_ready, 1)

            def gate_group(g, j):
                whole_out(GROUP0["gate"] + g, j, ps_z[:])
                dve.wait_ge(f_ready, j + (Z0["gate"] + g + 1))
                e = e_ft[:, bass.ds(j * GT + g * GT, GT)]
                nc.vector.tensor_tensor(e, e, s_buf[:], ALU.mult).then_inc(e_ready, 1)

            with dve.Fori(0, GD // 2 - 1) as n:
                for g in range(2):
                    splits(CHUNK0["gate"] + g * ND, n * (2 * ND))
                    gate_group(g, n * 2)
            for g in range(GD - 2, GD):
                splits(CHUNK0["gate"] + g * ND)
                gate_group(g, 0)

            dve.wait_ge(stat_done, 5)
            norm(3, D, RMS_EPS)
            for b in range(ND):
                for t in range(CK * b, CK * b + CK):
                    last = nc.vector.scalar_tensor_tensor(out=e_ft[:, t], in0=e_ft[:, t], scalar=vecs[:, V_PLEG + t:V_PLEG + t + 1],
                                                          in1=rstd[:], op0=ALU.mult, op1=ALU.mult)
                last.then_inc(o_step, 1)
                dve.wait_ge(o_step, b + 1)
                r = slice(CK * b, CK * b + CK)
                nc.vector.tensor_tensor(e_ft[:, r], e_ft[:, r], feat[:, r], ALU.add).then_inc(o_ready, 1)

        @block.tensor
        def _(pe):
            def products(c, dyn, g, operand, kt0, last_kt, i=0):
                slot, s = c % RING, 2 * (g % 2)
                for a in range(GT):
                    for k in range(CK):
                        kt = kt0 + k
                        nc.tensor.matmul(ps[:, s + a, :], w_hi[:, slot, k, a * P:a * P + P], operand[:, kt],
                                         start=(kt == 0), stop=False, skip_group_check=True)
                        last = nc.tensor.matmul(ps[:, s + a, T:], w_lo[:, slot, k, a * P:a * P + P], operand[:, kt, 0],
                                                start=False, stop=(kt == last_kt), skip_group_check=True)
                last.then_inc(w_used, 1)

            def group(c, dyn, g, gdyn, operand, nk=ND, block_ready=None, hook=None):
                if g >= 2 or not isinstance(gdyn, int):
                    pe.wait_ge(evacd, gdyn + (g - 1))
                for i in range(nk):
                    pe.wait_ge(w_lo_ready, dyn + (c + i + 1))
                    if block_ready is not None:
                        pe.wait_ge(mov_ready, block_ready + i + 1)
                    products(c + i, dyn, g, operand, CK * i, CK * nk - 1)
                    if hook:
                        hook(i)

            def total(src, n_src, out):
                for a in range(GT):
                    last = nc.tensor.matmul(out, ones_sb[:], src[:, a], start=(n_src == 0 and a == 0), stop=(a == 1),
                                            skip_group_check=True)
                return last

            bufs = (s_buf, g_buf, t_lo)
            pe.wait_ge(vec_landed, 32)
            for b in range(KT // 2):
                pe.wait_ge(sq_ready, b + 1)
                last = total(bufs[b % 3], b, ps_s[:, 0:T])
                last.then_inc(sq_used, 1)
            total_done = nc.tensor.matmul(ps_o[0:1, 0, 0:1], ones_sb[:, 0:1], ones_sb[:, 0:1], start=True, stop=True)
            total_done.then_inc(stat_done, 1)

            for g in range(2):
                group(g * ND, 0, g, 0, mov, block_ready=0 if g == 0 else None)

            def stage(name, n, hook=None):
                for g in range(2):
                    group(CHUNK0[name] + g * ND, n * (2 * ND), GROUP0[name] + g, n * 2, mov,
                          hook=(lambda i: hook(g * ND + i)) if hook else None)

            with pe.Fori(0, GA // 2) as n:
                stage("q", n)

            pe.wait_ge(evacd, 2)
            pe.wait_ge(att_landed, 32)
            for a, dst in enumerate((ps_t, ps_sc)):
                for c in range(NCH):
                    t0, nk = (c - 1) * CHUNK if c else 0, P if c else CHUNK
                    last = nc.tensor.transpose(dst[0:nk, c, :], kv_t[:, GT + a, t0:t0 + nk], ident_sb[:])
            last.then_inc(vt_done, 1)

            with pe.Fori(0, NKV) as n:
                def attention(pos):
                    for c in range(NCH):
                        t0, nk = (c - 1) * CHUNK if c else 0, P if c else CHUNK
                        if pos == TURN + STEP * c:
                            pe.wait_ge(p_norm, n * NCH + (c + 1))
                            for u in range(4):
                                last = nc.tensor.transpose(ps_t[:, u, :], probs[:, u, :], ident_sb[:])
                            last.then_inc(t_done, 1)
                        if pos == VALUES + STEP * c:
                            pe.wait_ge(vt_copied, 3)
                            pe.wait_ge(pt_ready, n * NCH + (c + 1))
                            pe.wait_ge(o_evacd, n * NCH + (c + 1))
                            for h in range(2):
                                last = nc.tensor.matmul(ps_o[HD * h:HD * h + HD, :, 0:CHUNK], v_st[0:nk, c, :],
                                                        probs_t[0:nk, 2 * h:2 * h + 2, :].rearrange("k a (b t) -> k (a b) t", t=CHUNK),
                                                        start=True, stop=True)
                            last.then_inc(pv_done, 1)
                    for c in range(NCH):
                        t0, nk = (c - 1) * CHUNK if c else 0, P if c else CHUNK
                        if pos == SCORES + STEP * c:
                            if c == 0:
                                pe.wait_ge(staged, n + 1)
                            for u in range(4):
                                h, pair = u // 2, u % 2
                                last = nc.tensor.matmul(score[u][:, 0:nk],
                                                        q_st[HD * h:HD * h + HD, c, 2 * pair:2 * pair + 2].rearrange("d a t -> d (a t)"),
                                                        k_st[HD * h:HD * h + HD, t0:t0 + nk], start=True, stop=True)
                            last.then_inc(sc_done, 1)

                stage("ca", n, attention)

            with pe.Fori(0, GA // 2) as n:
                stage("cb", n)
            with pe.Fori(0, GA // 2) as n:
                stage("ag", n)

            pe.wait_ge(b_done, GA)
            with pe.Fori(0, GD) as j:
                group(CHUNK0["attn"], j * (ND + NC_), GROUP0["attn"], j * 2, mov)
                group(CHUNK0["attn"] + ND, j * (ND + NC_), GROUP0["attn"] + 1, j * 2, branch, NC_)

            def layer_norm(i):
                if i == 0:
                    pe.wait_ge(sum_added, 1 + KC // 2)
                    total(sums, 0, ps_s[:, 0:T]).then_inc(stat_done, 1)
                if i == ND - 1:
                    pe.wait_ge(sum_added, SUM_LN + KC // 2)
                    total(sums, 0, ps_s[:, 0:T]).then_inc(stat_done, 1)

            group(CHUNK0["cg"], 0, GROUP0["cg"], 0, mov, hook=layer_norm)
            group(CHUNK0["cg"] + ND, 0, GROUP0["cg"] + 1, 0, mov)
            with pe.Fori(1, GA // 2) as n:
                stage("cg", n)

            pe.wait_ge(b_done, 2 * GA)
            with pe.Fori(0, GD) as j:
                group(CHUNK0["conv"], j * (ND + NC_), GROUP0["conv"], j * 2, mov)
                group(CHUNK0["conv"] + ND, j * (ND + NC_), GROUP0["conv"] + 1, j * 2, branch, NC_)

            group(CHUNK0["out"], 0, GROUP0["out"], 0, mov, block_ready=ND)
            group(CHUNK0["out"] + ND, 0, GROUP0["out"] + 1, 0, mov)
            with pe.Fori(1, GD // 2) as n:
                for g in range(2):
                    group(CHUNK0["out"] + g * ND, n * (2 * ND), GROUP0["out"] + g, n * 2, mov)

            pe.wait_ge(p_ready, 1)
            for i in range(GD // 2):
                c, g = CHUNK0["ple"] + i, GROUP0["ple"] + 2 * i
                pe.wait_ge(w_lo_ready, c + 1)
                for s in range(2):
                    pe.wait_ge(evacd, g + s - 1)
                    for a in range(GT):
                        for k in range(2):
                            col = (GT * s + a) * P
                            hi, lo = (w[:, c % RING, 2 * k + col // GW, col % GW:col % GW + P] for w in (w_hi, w_lo))
                            nc.tensor.matmul(ps[:, 2 * s + a, :], hi, p_mov[:, k], start=(k == 0), stop=False, skip_group_check=True)
                            last = nc.tensor.matmul(ps[:, 2 * s + a, T:], lo, p_mov[:, k, 0], start=False, stop=(k == 1),
                                                    skip_group_check=True)
                    last.then_inc(w_used if s else ple_half, 1)
                if i == 0:
                    pe.wait_ge(sum_added, SUM_OUT + GD)
                    total(sums, 0, ps_s[:, 0:T]).then_inc(stat_done, 1)

            group(CHUNK0["gate"], 0, GROUP0["gate"], 0, mov, block_ready=2 * ND)
            group(CHUNK0["gate"] + ND, 0, GROUP0["gate"] + 1, 0, mov)
            with pe.Fori(1, GD // 2) as n:
                for g in range(2):
                    group(CHUNK0["gate"] + g * ND, n * (2 * ND), GROUP0["gate"] + g, n * 2, mov)
            pe.wait_ge(sum_added, SUM_E + GD)
            total(sums, 0, ps_s[:, 0:T]).then_inc(stat_done, 1)


def kernel(**inputs):
    import concourse.bacc as bacc
    from concourse.bass_utils import run_bass_kernel_spmd

    def lay(name, shape=None):
        a = np.asarray(inputs[name])[0]
        return np.ascontiguousarray(a if shape is None else a.reshape(shape))

    def columns(name):
        return np.asarray(inputs[name])[0].reshape(-1, P).T

    taps = np.asarray(inputs["conv_w"])[0].reshape(TAPS, KC, P).transpose(2, 1, 0).reshape(P, KC * TAPS)
    vec = np.concatenate([columns(n) for n in ("b_in", "b_merge", "pre_norm_g", "post_norm_g", "ple_norm_g",
                                               "conv_b", "conv_ln_g", "conv_ln_b")] + [taps], axis=1)
    heads = np.asarray(inputs["attn_sinks"])[0].reshape(NKV, 2, 2, 2).transpose(2, 0, 3, 1).reshape(2, NKV * 4)
    arrays = {
        "xT": np.ascontiguousarray(np.asarray(inputs["x"])[0].T),
        "pT": np.ascontiguousarray(np.asarray(inputs["p"])[0, 0].T),
        "vec": np.ascontiguousarray(vec),
        "sinks": np.ascontiguousarray(np.repeat(heads, CHUNK, axis=0)),
        "ident": np.eye(P, dtype=np.float32),
        "ones": np.ones((P, P), np.float32),
        "w_in": lay("w_in"), "w_conv_out": lay("w_conv_out"), "w_attn_out": lay("w_attn_out"),
        "w_merge": lay("w_merge"), "w_out": lay("w_out"), "w_ple": lay("w_ple"), "w_gate": lay("w_ple_gate"),
    }
    nc = bacc.Bacc("TRN2", target_bir_lowering=False, num_devices=1)
    args = [nc.dram_tensor(f"{n}_dram", a.shape, mybir.dt.from_np(a.dtype), kind="ExternalInput").ap() for n, a in arrays.items()]
    out = nc.dram_tensor("outT_dram", (D, T), F32, kind="ExternalOutput").ap()
    build(nc, *args, out)
    r = run_bass_kernel_spmd(nc, [{f"{n}_dram": a for n, a in arrays.items()}], core_ids=[0])
    return np.ascontiguousarray(r.results[0]["outT_dram"].T)[None]
```

```python
from contextlib import ExitStack

import numpy as np

import concourse.bass as bass
from concourse import mybir

F32 = mybir.dt.float32
F32R = mybir.dt.float32r
ALU = mybir.AluOpType
ACT = mybir.ActivationFunctionType
AX_X = mybir.AxisListType.X

P = 128
T = 256
D = 4096
DC = 2048
DKV = 256
PLE = 256
CHUNK = 64
NQ, NKV, HD = 32, 4, 64
TAPS = 31
RMS_EPS, LN_EPS = 1e-6, 1e-5

KT = D // P
KC = DC // P
CK = 4
GT = 2
GW = GT * P
RING = 4
AHEAD = RING - 1
TAKEN = 2
ND = KT // CK
NC_ = KC // CK
GA = DC // GW
GD = D // GW
XB = 3
Y_EARLY = NC_
X1_FIRST = 2
UOFF = 2

CA0, CB0, CG0, Q0 = 0, DC, 2 * DC, 3 * DC
K0 = 4 * DC
AG0 = K0 + 2 * DKV
V_BIN, V_BM = 0, 84
V_PRE = V_BM + 64
V_POST, V_PLEG = V_PRE + 32, V_PRE + 64
V_CB, V_LG, V_LB = V_PRE + 96, V_PRE + 112, V_PRE + 128
V_CW = V_PRE + 144
V_ALL = V_CW + 16 * TAPS

STAGES = [("kv", 2, 2 * ND), ("q", GA, GA * ND), ("ca", GA, GA * ND), ("cb", GA, GA * ND), ("ag", GA, GA * ND),
          ("attn", 2 * GD, GD * (ND + NC_)), ("cg", GA, GA * ND), ("conv", 2 * GD, GD * (ND + NC_)),
          ("out", GD, GD * ND), ("ple", 0, GD // 2), ("gate", GD, GD * ND)]
CHUNK0, GROUP0 = {}, {}
_c = _g = 0
for _name, _groups, _chunks in STAGES:
    CHUNK0[_name], GROUP0[_name] = _c, _g
    _c, _g = _c + _chunks, _g + _groups
CHUNKS, GROUPS = _c, _g
NCH = T // CHUNK
STEP = 3
SCORES, TURN, VALUES = 1, 4, 6
ROW_MAX, SCALED, TURNED, HEADS = 2, 3, 5, 7
SUM_X = 1
SUM_MEAN = SUM_X + KT // 2 + 1
SUM_LN = SUM_MEAN + KC // 2 + 1
SUM_OUT = SUM_LN + KC // 2 + 1
SUM_E = SUM_OUT + GD + 1
NORM_STEPS = 5
H0 = {"kv": 0, "q": 2, "ca": 2 + GA, "cb": 2 + 2 * GA, "ag": 2 + 3 * GA, "attn": 2 + 4 * GA, "cg": 2 + 4 * GA + GD,
      "conv": 2 + 5 * GA + GD}
Z0 = {"cb": 0, "ag": GA, "attn": 2 * GA, "cg": 2 * GA + GD, "conv": 3 * GA + GD, "gate": 3 * GA + 2 * GD}


def build(nc, xT, pT, vec, sinks, ident, ones, w_in, w_conv_out, w_attn_out, w_merge, w_out, w_ple, w_gate, outT):
    with ExitStack() as ctx:
        def sb(name, shape, dt, where=ctx):
            return where.enter_context(nc.sbuf_tensor(name, shape, dt))

        def sem(name):
            return ctx.enter_context(nc.semaphore(name))

        w_raw = sb("w_raw", [P, RING, CK, GW], F32)
        w_hi = sb("w_hi", [P, RING, CK, GW], F32R)
        w_lo = sb("w_lo", [P, RING, CK, GW], F32R)
        mov = sb("mov", [P, KT, 2, T], F32R)
        feat = sb("feat", [P, KT, T], F32)
        vecs = sb("vecs", [P, V_ALL], F32)
        ones_sb = sb("ones_sb", [P, P], F32)
        t_lo = sb("t_lo", [P, GT, T], F32)
        s_buf = sb("s_buf", [P, GT, T], F32)
        g_buf = sb("g_buf", [P, GT, T], F32)
        sums = sb("sums", [P, GT, T], F32)
        rstd = sb("rstd", [P, T], F32)
        h_rstd = sb("h_rstd", [P, T], F32)
        with ExitStack() as u_ctx:
            x_blk = sb("x_blk", [P, XB, CK, T], F32, u_ctx)
            p_raw = sb("p_raw", [P, 2, T], F32, u_ctx)
            p_mov = sb("p_mov", [P, 2, 2, T], F32R, u_ctx)
        conv = sb("conv", [P, KC + UOFF, T], F32)
        with ExitStack() as z_ctx:
            x_in = sb("x_in", [P, KT, T], F32, z_ctx)
        with ExitStack() as z_ctx:
            kv_t = sb("kv_t", [P, 2 * GT, T], F32, z_ctx)
            k_dup = sb("k_dup", [P, NKV, T], F32, z_ctx)
            v_tok = sb("v_tok", [P, NCH, DKV], F32, z_ctx)
            q_st = sb("q_st", [P, NCH, 4, CHUNK], F32, z_ctx)
            k_st = sb("k_st", [P, T], F32, z_ctx)
            v_st = sb("v_st", [P, NCH, HD], F32, z_ctx)
            probs = sb("probs", [P, 4, P], F32, z_ctx)
            probs_t = sb("probs_t", [P, 4, P], F32, z_ctx)
            sink = sb("sink", [P, NKV, 4], F32, z_ctx)
            nsink = sb("nsink", [P, NKV, 4], F32, z_ctx)
            ident_sb = sb("ident_sb", [P, P], F32, z_ctx)
            negm = sb("negm", [P, 4], F32, z_ctx)
            smax = sb("smax", [P, 4], F32, z_ctx)
            rowsum = sb("rowsum", [P, 4], F32, z_ctx)
            sdiff = sb("sdiff", [P, 4], F32, z_ctx)
            esink = sb("esink", [P, 4], F32, z_ctx)
            denom = sb("denom", [P, 4], F32, z_ctx)
            rden = sb("rden", [P, 4], F32, z_ctx)
        with ExitStack() as z_ctx:
            branch = sb("branch", [P, KC, 2, T], F32R, z_ctx)
        e_ft = sb("e_ft", [P, KT, T], F32)

        def bank(name, shape):
            return ctx.enter_context(nc.psum_tensor(name, shape, F32))

        ps = bank("ps", [P, 4, 2 * T])
        ps_z = bank("ps_z", [P, GT, T])
        ps_sc = ps_z[:, :, :].rearrange("p a b -> p (a b)").rearrange("p (u k) -> p u k", u=4)
        ps_t = bank("ps_t", [P, 4, P])
        ps_o = bank("ps_o", [P, 4, 2 * CHUNK])
        ps_s = bank("ps_s", [P, 2 * T])

        ps_sc2 = ps_s[:, :].rearrange("p (u k) -> p u k", u=4)
        score = [ps_sc[:, 0], ps_sc[:, 1], ps_sc2[:, 0], ps_sc2[:, 1]]

        x_landed = [sem(f"x_landed{i}") for i in range(ND)]
        ones_landed, vec_landed, taps_landed, att_landed, kd_landed, p_landed = (
            sem(n) for n in ("ones_landed", "vec_landed", "taps_landed", "att_landed", "kd_landed", "p_landed"))
        xb_landed = [sem(f"xb_landed{i}") for i in range(XB)]
        w_landed = [sem(f"w_landed{i}") for i in range(RING)]
        w_hi_ready, w_lo_ready, w_used = sem("w_hi_ready"), sem("w_lo_ready"), sem("w_used")
        lo_out, evacd = sem("lo_out"), sem("evacd")
        f_ready = sem("f_ready")
        ple_half, ple_out = sem("ple_half"), sem("ple_out")
        xg_ready, yg_ready, eg_ready = sem("xg_ready"), sem("yg_ready"), sem("eg_ready")
        sq_ready = sem("sq_ready")
        xg_hi, mov_ready, y_hi = sem("xg_hi"), sem("mov_ready"), sem("y_hi")
        scaled, kv_ready = sem("scaled"), sem("kv_ready")
        x1_part, x1_ready, x1_hi = sem("x1_part"), sem("x1_ready"), sem("x1_hi")
        p_hi, p_ready = sem("p_hi"), sem("p_ready")
        u_done = sem("u_done")
        b_ready, b_hi, b_done = sem("b_ready"), sem("b_hi"), sem("b_done")
        y_done = sem("y_done")
        conv_init, conv_tap = sem("conv_init"), sem("conv_tap")
        ln_mean, ln_cent, ln_ready, ln_act = sem("ln_mean"), sem("ln_cent"), sem("ln_ready"), sem("ln_act")
        sum_in, sum_added, stat_done = sem("sum_in"), sem("sum_added"), sem("stat_done")
        norm_step, root_ready = sem("norm_step"), sem("root_ready")
        e_ready, o_step, o_stored = sem("e_ready"), sem("o_step"), sem("o_stored")
        o_ready = [sem("o_ready_dve"), sem("o_ready_pool")]
        vt_done, vt_copied, staged = sem("vt_done"), sem("vt_copied"), sem("staged")
        sc_done, att_step, m_ready, p_exp, p_norm = (sem(n) for n in ("sc_done", "att_step", "m_ready", "p_exp", "p_norm"))
        t_done, pt_ready, pv_done, o_evacd = sem("t_done"), sem("pt_ready"), sem("pv_done"), sem("o_evacd")

        xT_v = xT.rearrange("(k p) t -> p k t", p=P)
        outT_v = outT.rearrange("(k p) t -> p k t", p=P)
        rows = {n: w.rearrange("(k p) n -> p k n", p=P) for n, w in
                (("in", w_in), ("merge", w_merge), ("attn", w_attn_out), ("conv", w_conv_out),
                 ("out", w_out), ("ple", w_ple), ("gate", w_gate))}

        block = ctx.enter_context(nc.Block())

        @block.sync
        def _(sp):
            def load_chunk(c, dyn, w, k0, col):
                if isinstance(dyn, int) and c + dyn < RING:
                    pass
                else:
                    sp.wait_ge(w_lo_ready, dyn + (c - RING + 1))
                sp.dma_start(w_raw[:, c % RING], rows[w][:, k0:k0 + CK, bass.ds(col, GW)]).then_inc(w_landed[c % RING], 16)

            def load_group(c, dyn, w, col, nk=ND):
                for i in range(nk):
                    load_chunk(c + i, dyn, w, CK * i, col)

            def load_stage(name, col0):
                with sp.Fori(0, GA // 2) as n:
                    for g in range(2):
                        load_group(CHUNK0[name] + g * ND, n * (2 * ND), "in", n * (2 * GW) + (col0 + g * GW))

            for b in range(ND):
                sp.dma_start(x_in[:, CK * b:CK * b + CK], xT_v[:, CK * b:CK * b + CK]).then_inc(x_landed[b], 16)
                if b == 0:
                    sp.dma_start(ones_sb[:], ones).then_inc(ones_landed, 16)
                    sp.dma_start(vecs[:, 0:V_CW], vec[:, 0:V_CW]).then_inc(vec_landed, 16)
                for g in range(2):
                    load_chunk(2 * b + g, 0, "in", CK * b, K0 + g * GW)
            load_stage("q", Q0)
            sp.wait_ge(kv_ready, 1)
            sp.dma_start(vecs[:, V_CW:], vec[:, V_CW:]).then_inc(taps_landed, 16)
            sp.dma_start(ident_sb[:], ident).then_inc(att_landed, 16)
            sp.dma_start(sink[:], sinks.rearrange("p (n u) -> p n u", u=4)).then_inc(att_landed, 16)
            for e in range(2):
                for half in range(2):
                    sp.dma_start(k_dup[HD * half:HD * half + HD, e:NKV:2, :],
                                 kv_t[HD * e:HD * e + HD, 0:GT, :]).then_inc(kd_landed, 16)
            load_stage("ca", CA0)
            load_stage("cb", CB0)
            load_stage("ag", AG0)
            with sp.Fori(1, GD + 1) as j:
                c = CHUNK0["attn"] - (ND + NC_)
                load_group(c, j * (ND + NC_), "merge", j * GW + (D - GW))
                load_group(c + ND, j * (ND + NC_), "attn", j * GW - GW, NC_)
            load_stage("cg", CG0)
            with sp.Fori(0, GD) as j:
                load_group(CHUNK0["conv"], j * (ND + NC_), "merge", j * GW)
                load_group(CHUNK0["conv"] + ND, j * (ND + NC_), "conv", j * GW, NC_)
            sp.wait_ge(evacd, GROUP0["conv"])
            sp.dma_start(p_raw[:], pT.rearrange("(k p) t -> p k t", p=P)).then_inc(p_landed, 16)
            for b in range(XB):
                sp.dma_start(x_blk[:, b], xT_v[:, CK * b:CK * b + CK]).then_inc(xb_landed[b], 16)
            with sp.Fori(0, GD) as j:
                load_group(CHUNK0["out"], j * ND, "out", j * GW)
            with sp.Fori(0, 2) as n:
                for i in range(RING):
                    c = CHUNK0["ple"] + i
                    sp.wait_ge(w_lo_ready, n * RING + (c - RING + 1))
                    sp.dma_start(w_raw[:, c % RING].rearrange("p a b -> p (a b)").rearrange("p (k n) -> p k n", k=2),
                                 rows["ple"][:, :, bass.ds(n * (RING * 2 * GW) + i * 2 * GW, 2 * GW)]
                                 ).then_inc(w_landed[c % RING], 16)
            with sp.Fori(0, GD) as j:
                load_group(CHUNK0["gate"], j * ND, "gate", j * GW)
            for b in range(ND):
                sp.wait_ge(o_ready[b % 2], b // 2 + 1)
                sp.dma_start(outT_v[:, CK * b:CK * b + CK], e_ft[:, CK * b:CK * b + CK]).then_inc(o_stored, 16)
            sp.wait_ge(o_stored, 16 * ND)

        @block.gpsimd
        def _(pool):
            def clear(done):
                pool.wait_ge(stat_done, done)
                nc.gpsimd.memset(sums[:], 0.0).then_inc(sum_added, 1)

            def add(src, n):
                pool.wait_ge(sum_added, n)
                nc.gpsimd.tensor_tensor(sums[:], sums[:], src, ALU.add).then_inc(sum_added, 1)

            nc.gpsimd.memset(sums[:], 0.0).then_inc(sum_added, 1)
            for i in range(KT // 2):
                pool.wait_ge(sq_ready, i + 1)
                add((s_buf, g_buf, t_lo)[i % 3][:], SUM_X + i)
            clear(1)
            with pool.Fori(0, KC // 2) as i:
                pool.wait_ge(conv_tap, i * (2 * (TAPS - 1)) + 2 * (TAPS - 1))
                add(conv[:, bass.ds(i * 2, 2)], i + SUM_MEAN)
            clear(2)
            for i in range(KC // 2):
                pool.wait_ge(sum_in, i + 1)
                add((s_buf, g_buf)[i % 2][:], SUM_LN + i)
            clear(3)
            with pool.Fori(0, GD) as j:
                pool.wait_ge(sum_in, j + (KC // 2 + 1))
                add(s_buf[:], j + SUM_OUT)
            clear(4)
            for i in range(ND):
                pool.wait_ge(x1_part, i + 1)
                pool.wait_ge(xb_landed[i % XB], 16 * (i // XB + 1))
                r = slice(CK * i, CK * i + CK)
                nc.gpsimd.tensor_tensor(feat[:, r], feat[:, r], x_blk[:, i % XB], ALU.add).then_inc(x1_ready, 1)
            with pool.Fori(0, GD) as j:
                pool.wait_ge(sum_in, j + (KC // 2 + GD + 1))
                add(s_buf[:], j + SUM_E)
            for b in range(1, ND, 2):
                pool.wait_ge(o_step, b + 1)
                r = slice(CK * b, CK * b + CK)
                nc.gpsimd.tensor_tensor(e_ft[:, r], e_ft[:, r], feat[:, r], ALU.add).then_inc(o_ready[1], 1)

        @block.scalar
        def _(act):
            def split(c, dyn=0):
                act.wait_ge(w_landed[c % RING], dyn * 16 // RING + 16 * (c // RING + 1) if isinstance(dyn, int)
                            else dyn * (16 // RING) + 16 * (c // RING + 1))
                if c >= RING or not isinstance(dyn, int):
                    act.wait_ge(w_used, dyn + (c - RING + 1))
                nc.scalar.copy(w_hi[:, c % RING], w_raw[:, c % RING]).then_inc(w_hi_ready, 1)

            def split_at(c, dyn=0):
                if c + AHEAD < CHUNKS:
                    split(c + AHEAD, dyn)

            def splits(c, dyn=0, nk=ND, hook=None, first=None, taken=TAKEN):
                for i in range(nk):
                    if first:
                        first(i)
                    if i >= taken:
                        split_at(c + i, dyn)
                    if hook:
                        hook(i)

            def between(end, dyn, *steps):
                for i in range(TAKEN):
                    split_at(end + i, dyn)
                    if i < len(steps):
                        steps[i]()

            def half_out(g, gdyn, c_end, cdyn):
                act.wait_ge(w_used, cdyn + c_end)
                if g > 0 or not isinstance(gdyn, int):
                    act.wait_ge(evacd, gdyn + g)
                nc.scalar.copy(t_lo[:], ps[:, 2 * (g % 2):2 * (g % 2) + 2, T:]).then_inc(lo_out, 1)

            def function(h, hdyn, dst, f, bias):
                act.wait_ge(scaled, hdyn + (h + 1))
                for a in range(GT):
                    last = nc.scalar.activation(dst[:, a], ps_z[:, a], f, bias=vecs[:, bass.ds(bias + a, 1)])
                last.then_inc(f_ready, 1)

            act.wait_ge(ones_landed, 16)
            nc.scalar.activation(rstd[:, 0:1], ones_sb[:, 0:1], ACT.Sqrt)
            def squares(b):
                act.wait_ge(x_landed[b], 16)
                for i in (2 * b, 2 * b + 1):
                    if i >= 3:
                        act.wait_ge(sum_added, SUM_X + i - 2)
                    nc.scalar.activation((s_buf, g_buf, t_lo)[i % 3][:], x_in[:, 2 * i:2 * i + 2], ACT.Square).then_inc(sq_ready, 1)

            def xg_high(b):
                act.wait_ge(xg_ready, b + 1)
                nc.scalar.copy(mov[:, CK * b:CK * b + CK, 0], x_in[:, CK * b:CK * b + CK]).then_inc(xg_hi, 1)

            squares(0)
            split(0)
            xg_high(0)
            split(1)
            squares(1)
            split(2)
            xg_high(1)

            def kv_hook(i):
                if i // 2 + 2 < ND:
                    (xg_high if i % 2 else squares)(i // 2 + 2)
                if i == 2 * ND - 3:
                    act.wait_ge(norm_step, 2)
                    nc.scalar.activation(h_rstd[:], h_rstd[:], ACT.Sqrt).then_inc(root_ready, 1)
                if i >= 2 * ND - 2:
                    half_out(i - (2 * ND - 2), 0, i + 1, 0)

            splits(0, nk=2 * ND, hook=kv_hook, taken=0)

            with act.Fori(0, GA // 2) as n:
                for g in range(2):
                    splits(CHUNK0["q"] + g * ND, n * (2 * ND), taken=0)
                    half_out(GROUP0["q"] + g, n * 2, CHUNK0["q"] + (g + 1) * ND, n * (2 * ND))

            with act.Fori(0, NKV) as n:
                def attention(pos):
                    for c in range(NCH):
                        nk = P if c else CHUNK
                        if pos == ROW_MAX + STEP * c:
                            act.wait_ge(m_ready, n * NCH + (c + 1))
                            for u in range(4):
                                nc.scalar.activation(probs[:, u, 0:nk], score[u][:, 0:nk], ACT.Exp, bias=negm[:, u:u + 1],
                                                     scale=HD ** -0.5, accum_out=rowsum[:, u:u + 1])
                            nc.scalar.activation(esink[:], sdiff[:], ACT.Exp).then_inc(p_exp, 1)
                        if pos == TURNED + STEP * c:
                            act.wait_ge(t_done, n * NCH + (c + 1))
                            nc.scalar.copy(probs_t[0:nk], ps_t[0:nk]).then_inc(pt_ready, 1)

                for g in range(2):
                    splits(CHUNK0["ca"] + g * ND, n * (2 * ND), hook=lambda i: attention(g * ND + i), taken=0)
                    half_out(GROUP0["ca"] + g, n * 2, CHUNK0["ca"] + (g + 1) * ND, n * (2 * ND))

            between(CHUNK0["cb"], 0)
            with act.Fori(0, GA // 2) as n:
                for g in range(2):
                    splits(CHUNK0["cb"] + g * ND, n * (2 * ND))
                    half_out(GROUP0["cb"] + g, n * 2, CHUNK0["cb"] + (g + 1) * ND, n * (2 * ND))
                    between(CHUNK0["cb"] + (g + 1) * ND, n * (2 * ND), lambda: function(
                        H0["cb"] + g, n * 2, s_buf, ACT.Sigmoid, n * (2 * GT) + (V_BIN + CB0 // P + g * GT)))

            with act.Fori(0, GA // 2) as n:
                for g in range(2):
                    splits(CHUNK0["ag"] + g * ND, n * (2 * ND))
                    half_out(GROUP0["ag"] + g, n * 2, CHUNK0["ag"] + (g + 1) * ND, n * (2 * ND))
                    tile = n * (2 * GT) + g * GT

                    def gated_high():
                        act.wait_ge(b_ready, n * 2 + (g + 1))
                        nc.scalar.copy(branch[:, bass.ds(tile, GT), 0], feat[:, bass.ds(tile, GT)]).then_inc(b_hi, 1)

                    between(CHUNK0["ag"] + (g + 1) * ND, n * (2 * ND),
                            lambda: function(H0["ag"] + g, n * 2, s_buf, ACT.Silu, tile + (V_BIN + AG0 // P)), gated_high)

            with act.Fori(0, GD // 2) as i:
                act.wait_ge(u_done, GA)
                act.wait_ge(taps_landed, 16)
                act.wait_ge(sum_added, i + SUM_MEAN)
                for a in range(2):
                    nc.scalar.activation(conv[:, bass.ds(i * 2 + a, 1)], conv[:, bass.ds(i * 2 + (a + UOFF), 1)], ACT.Identity,
                                         bias=vecs[:, bass.ds(i * 2 + (V_CB + a), 1)],
                                         scale=vecs[:, bass.ds(i * (2 * TAPS) + (V_CW + a * TAPS + TAPS - 1), 1)]
                                         ).then_inc(conv_init, 1)
                for jj in range(2):
                    c, g = CHUNK0["attn"] + jj * (ND + NC_), GROUP0["attn"] + 2 * jj
                    cd, gd = i * (2 * (ND + NC_)), i * 4
                    splits(c, cd)
                    half_out(g, gd, c + ND, cd)
                    between(c + ND, cd, lambda: function(
                        H0["attn"] + jj, i * 2, g_buf, ACT.Sigmoid, i * (2 * GT) + (V_BM + KT + jj * GT)))
                    splits(c + ND, cd, NC_)
                    half_out(g + 1, gd, c + ND + NC_, cd)
                    between(c + ND + NC_, cd)

            def conv_gate(n, g):
                tile = n * (2 * GT) + g * GT
                act.wait_ge(ln_ready, n * 2 + (g + 1))
                for a in range(GT):
                    nc.scalar.activation(g_buf[:, a], s_buf[:, a], ACT.Silu, bias=vecs[:, bass.ds(tile + (V_LB + a), 1)],
                                         scale=vecs[:, bass.ds(tile + (V_LG + a), 1)]).then_inc(ln_act, 1)
                half_out(GROUP0["cg"] + g, n * 2, CHUNK0["cg"] + (g + 1) * ND, n * (2 * ND))

                def gated_high():
                    act.wait_ge(b_ready, n * 2 + (GA + g + 1))
                    nc.scalar.copy(branch[:, bass.ds(tile, GT), 0], g_buf[:]).then_inc(b_hi, 1)

                between(CHUNK0["cg"] + (g + 1) * ND, n * (2 * ND),
                        lambda: function(H0["cg"] + g, n * 2, s_buf, ACT.Silu, tile + (V_BIN + CG0 // P)), gated_high)

            def ln_squares(pos):
                for i in (2 * pos - 4, 2 * pos - 3) if 2 <= pos < 6 else ():
                    act.wait_ge(ln_cent, i + 1)
                    if i >= 2:
                        act.wait_ge(sum_added, SUM_LN + i - 1)
                    nc.scalar.activation((s_buf, g_buf)[i % 2][:], conv[:, 2 * i:2 * i + 2], ACT.Square).then_inc(sum_in, 1)

            def ln_root(pos):
                if pos == ND - 1:
                    act.wait_ge(norm_step, NORM_STEPS + 2)
                    nc.scalar.activation(rstd[:], rstd[:], ACT.Sqrt).then_inc(root_ready, 1)

            splits(CHUNK0["cg"], hook=lambda i: (ln_squares(i), ln_root(i)))
            conv_gate(0, 0)
            splits(CHUNK0["cg"] + ND)
            conv_gate(0, 1)
            with act.Fori(1, GA // 2) as n:
                for g in range(2):
                    splits(CHUNK0["cg"] + g * ND, n * (2 * ND))
                    conv_gate(n, g)

            def y_high(i):
                if i >= ND:
                    return
                act.wait_ge(y_done, GD + 2 * 2 * (i + 1))
                nc.scalar.copy(mov[:, CK * i:CK * i + CK, 0], feat[:, CK * i:CK * i + CK]).then_inc(y_hi, 1)

            def conv_out(j, late=None):
                c, g = CHUNK0["conv"], GROUP0["conv"]
                splits(c, j * (ND + NC_))
                half_out(g, j * 2, c + ND, j * (ND + NC_))
                between(c + ND, j * (ND + NC_), lambda: function(H0["conv"], j, g_buf, ACT.Sigmoid, j * GT + V_BM))
                splits(c + ND, j * (ND + NC_), NC_, hook=late)
                half_out(g + 1, j * 2, c + ND + NC_, j * (ND + NC_))
                between(c + ND + NC_, j * (ND + NC_))

            with act.Fori(0, GD - 1) as j:
                conv_out(j)
            conv_out(GD - 1, y_high)

            def out_group(g, j):
                half_out(GROUP0["out"] + g, j, CHUNK0["out"] + (g + 1) * ND, j * ND)
                act.wait_ge(evacd, j + (GROUP0["out"] + g + 1))
                act.wait_ge(sum_added, j + (SUM_OUT + g))
                nc.scalar.activation(s_buf[:], feat[:, bass.ds(j * GT + g * GT, GT)], ACT.Square).then_inc(sum_in, 1)
                act.wait_ge(sum_in, j + (KC // 2 + g + 1))
                for a in range(GT):
                    y = feat[:, bass.ds(j * GT + (g * GT + a), 1)]
                    nc.scalar.activation(y, y, ACT.Identity, scale=vecs[:, bass.ds(j * GT + (V_POST + g * GT + a), 1)]
                                         ).then_inc(yg_ready, 1)
                between(CHUNK0["out"] + (g + 1) * ND, j * ND)

            splits(CHUNK0["out"], first=lambda i: y_high(i + Y_EARLY))
            out_group(0, 0)
            splits(CHUNK0["out"] + ND)
            out_group(1, 0)
            act.wait_ge(p_landed, 16)
            nc.scalar.copy(p_mov[:, :, 0], p_raw[:]).then_inc(p_hi, 1)
            with act.Fori(1, GD // 2) as n:
                for g in range(2):
                    splits(CHUNK0["out"] + g * ND, n * (2 * ND))
                    out_group(g, n * 2)

            def x1_high(i):
                if not 0 <= i < ND:
                    return
                act.wait_ge(x1_ready, i + 1)
                nc.scalar.copy(mov[:, CK * i:CK * i + CK, 0], feat[:, CK * i:CK * i + CK]).then_inc(x1_hi, 1)
                if i + XB < ND:
                    act.dma_start(x_blk[:, i % XB], xT_v[:, CK * (i + XB):CK * (i + XB + 1)]).then_inc(xb_landed[i % XB], 16)

            for i in range(GD // 2):
                if i == X1_FIRST:
                    act.wait_ge(norm_step, 2 * NORM_STEPS + 2)
                    nc.scalar.activation(rstd[:], rstd[:], ACT.Sqrt).then_inc(root_ready, 1)
                x1_high(i - X1_FIRST - 1)
                if i >= TAKEN:
                    split_at(CHUNK0["ple"] + i)
                act.wait_ge(ple_half, i + 1)
                nc.scalar.copy(e_ft[:, CK * i:CK * i + GT], ps[:, 0:2, 0:T]).then_inc(ple_out, 1)
                act.wait_ge(w_used, CHUNK0["ple"] + i + 1)
                nc.scalar.copy(e_ft[:, CK * i + GT:CK * i + CK], ps[:, 2:4, 0:T]).then_inc(ple_out, 1)

            def gate_group(g, j):
                half_out(GROUP0["gate"] + g, j, CHUNK0["gate"] + (g + 1) * ND, j * ND)
                split_at(CHUNK0["gate"] + (g + 1) * ND, j * ND)
                act.wait_ge(sum_added, j + (SUM_E + g))
                act.wait_ge(evacd, j + (GROUP0["gate"] + g + 1))
                nc.scalar.activation(s_buf[:], ps_z[:], ACT.Sigmoid).then_inc(f_ready, 1)
                split_at(CHUNK0["gate"] + (g + 1) * ND + 1, j * ND)
                act.wait_ge(e_ready, j + (g + 1))
                nc.scalar.activation(s_buf[:], e_ft[:, bass.ds(j * GT + g * GT, GT)], ACT.Square).then_inc(sum_in, 1)
                act.wait_ge(sum_in, j + (KC // 2 + GD + g + 1))
                for a in range(GT):
                    e = e_ft[:, bass.ds(j * GT + (g * GT + a), 1)]
                    nc.scalar.activation(e, e, ACT.Identity, scale=vecs[:, bass.ds(j * GT + (V_PLEG + g * GT + a), 1)]
                                         ).then_inc(eg_ready, 1)

            splits(CHUNK0["gate"], first=lambda i: x1_high(GD // 2 + i - X1_FIRST - 1), taken=0)
            gate_group(0, 0)
            splits(CHUNK0["gate"] + ND)
            gate_group(1, 0)
            with act.Fori(1, GD // 2 - 1) as n:
                for g in range(2):
                    splits(CHUNK0["gate"] + g * ND, n * (2 * ND))
                    gate_group(g, n * 2)
            for g in range(GD - 2, GD):
                splits(CHUNK0["gate"] + g * ND)
                gate_group(g, 0)
            act.wait_ge(norm_step, 3 * NORM_STEPS + 2)
            nc.scalar.activation(rstd[:], rstd[:], ACT.Sqrt).then_inc(root_ready, 1)

        @block.vector
        def _(dve):
            def split(c, dyn=0):
                dve.wait_ge(w_hi_ready, dyn + (c + 1))
                nc.vector.tensor_tensor(w_lo[:, c % RING], w_raw[:, c % RING], w_hi[:, c % RING].bitcast(F32),
                                        ALU.subtract).then_inc(w_lo_ready, 1)

            def split_at(c, dyn=0):
                if c + AHEAD < CHUNKS:
                    split(c + AHEAD, dyn)

            def splits(c, dyn=0, nk=ND, hook=None, first=None, taken=TAKEN):
                for i in range(nk):
                    if first:
                        first(i)
                    if i >= taken:
                        split_at(c + i, dyn)
                    if hook:
                        hook(i)

            def between(end, dyn, *steps):
                for i in range(TAKEN):
                    split_at(end + i, dyn)
                    if i < len(steps):
                        steps[i]()

            def whole_out(g, gdyn, dst):
                dve.wait_ge(lo_out, gdyn + (g + 1))
                s = 2 * (g % 2)
                nc.vector.tensor_tensor(dst, ps[:, s:s + 2, 0:T], t_lo[:], ALU.add).then_inc(evacd, 1)

            def h_out(g, gdyn, dst):
                whole_out(g, gdyn, dst)
                dve.wait_ge(evacd, gdyn + (g + 1))
                nc.vector.tensor_tensor(dst, dst, over_tiles(GT, h_rstd), ALU.mult).then_inc(scaled, 1)

            def norm(k, n, eps, rstd=rstd):
                v, w = g_buf[:, 0], g_buf[:, 1]
                s = k * NORM_STEPS
                nc.vector.tensor_scalar(v, ps_s[:, 0:T], 1.0 / n, eps, ALU.mult, ALU.add).then_inc(norm_step, 1)
                dve.wait_ge(norm_step, s + 1)
                nc.vector.reciprocal(rstd[:], v).then_inc(norm_step, 1)
                dve.wait_ge(root_ready, k + 1)
                nc.vector.tensor_tensor(w, rstd[:], rstd[:], ALU.mult).then_inc(norm_step, 1)
                dve.wait_ge(norm_step, s + 3)
                nc.vector.scalar_tensor_tensor(out=w, in0=w, scalar=-0.5, in1=v, op0=ALU.mult, op1=ALU.mult).then_inc(norm_step, 1)
                dve.wait_ge(norm_step, s + 4)
                nc.vector.scalar_tensor_tensor(out=rstd[:], in0=w, scalar=1.5, in1=rstd[:], op0=ALU.add, op1=ALU.mult
                                               ).then_inc(norm_step, 1)
                dve.wait_ge(norm_step, s + 5)

            def low(dst, whole, high):
                return nc.vector.tensor_tensor(dst, whole, high.bitcast(F32), ALU.subtract)

            def over_tiles(k, rstd=rstd):
                return rstd[:].unsqueeze(1).to_broadcast([P, k, T])

            def gain(b):
                dve.wait_ge(sq_ready, 2 * b + 2)
                for t in range(CK * b, CK * b + CK):
                    last = nc.vector.tensor_scalar(x_in[:, t], x_in[:, t], vecs[:, V_PRE + t:V_PRE + t + 1], None, ALU.mult)
                last.then_inc(xg_ready, 1)

            def xg_low(b):
                dve.wait_ge(xg_hi, b + 1)
                r = slice(CK * b, CK * b + CK)
                low(mov[:, r, 1], x_in[:, r], mov[:, r, 0]).then_inc(mov_ready, 1)

            dve.wait_ge(vec_landed, 16)
            gain(0)
            split(0)
            xg_low(0)
            split(1)
            gain(1)
            split(2)
            xg_low(1)

            def kv_hook(i):
                if i // 2 + 2 < ND:
                    (xg_low if i % 2 else gain)(i // 2 + 2)
                if i == 2 * ND - 3:
                    dve.wait_ge(stat_done, 1)
                    norm(0, D, RMS_EPS, h_rstd)
                if i >= 2 * ND - 2:
                    g = i - (2 * ND - 2)
                    h_out(g, 0, kv_t[:, GT * g:GT * g + GT])
                    dve.wait_ge(scaled, g + 1)
                    for a in range(GT * g, GT * g + GT):
                        bias = V_BIN + K0 // P + a
                        last = nc.vector.tensor_scalar(kv_t[:, a], kv_t[:, a], vecs[:, bias:bias + 1], None, ALU.add)
                    last.then_inc(kv_ready, 1)

            splits(0, nk=2 * ND, hook=kv_hook, taken=0)

            with dve.Fori(0, GA // 2) as n:
                for g in range(2):
                    splits(CHUNK0["q"] + g * ND, n * (2 * ND), taken=0)
                    h_out(GROUP0["q"] + g, n * 2, feat[:, bass.ds(n * (2 * GT) + g * GT, GT)])

            dve.wait_ge(vt_done, 1)
            for a, src in enumerate((ps_t, ps_sc)):
                nc.vector.tensor_copy(v_tok[0:CHUNK, 0, a * P:a * P + P], src[0:CHUNK, 0])
                nc.vector.tensor_copy(v_tok[:, 1:NCH, a * P:a * P + P], src[:, 1:NCH]).then_inc(vt_copied, 1)
            dve.wait_ge(att_landed, 32)
            nc.vector.tensor_scalar(nsink[:], sink[:], -1.0, None, ALU.mult).then_inc(vt_copied, 1)
            nc.vector.memset(probs[:], 0.0).then_inc(o_evacd, 1)
            dve.wait_ge(vt_copied, 3)
            dve.wait_ge(kd_landed, 64)
            dve.wait_ge(scaled, H0["ca"])

            with dve.Fori(0, NKV) as n:
                for a in range(4):
                    nc.vector.tensor_scalar(q_st[:, :, a], feat[:, bass.ds(n * 4 + a, 1)].rearrange("p a (c t) -> p (a c) t", t=CHUNK),
                                            vecs[:, bass.ds(n * 4 + (V_BIN + Q0 // P + a), 1)], None, ALU.add)
                nc.vector.tensor_copy(k_st[:], k_dup[:, bass.ds(n, 1)])
                nc.vector.tensor_copy(v_st[0:CHUNK, 0:1], v_tok[0:CHUNK, 0:1, bass.ds(n * HD, HD)])
                nc.vector.tensor_copy(v_st[:, 1:NCH], v_tok[:, 1:NCH, bass.ds(n * HD, HD)]).then_inc(staged, 1)

                def head_out(c):
                    dve.wait_ge(pv_done, n * NCH + (c + 1))
                    nc.vector.tensor_scalar(feat[:, bass.ds(n * 4, 4), c * CHUNK:(c + 1) * CHUNK], ps_o[:, :, 0:CHUNK], 1.0, None,
                                            ALU.mult).then_inc(o_evacd, 1)

                def attention(pos):
                    for c in range(NCH):
                        nk = P if c else CHUNK
                        s, st = n * (4 * NCH), 4 * c
                        if pos == ROW_MAX + STEP * c:
                            dve.wait_ge(sc_done, n * NCH + (c + 1))
                            nc.vector.tensor_reduce(smax[:, 0:2], ps_sc[:, 0:2, 0:nk], AX_X, ALU.max)
                            nc.vector.tensor_reduce(smax[:, 2:4], ps_sc2[:, 0:2, 0:nk], AX_X, ALU.max).then_inc(att_step, 1)
                            dve.wait_ge(att_step, s + (st + 1))
                            nc.vector.scalar_tensor_tensor(out=negm[:], in0=smax[:], scalar=-(HD ** -0.5), in1=nsink[:, bass.ds(n, 1)],
                                                           op0=ALU.mult, op1=ALU.min).then_inc(att_step, 1)
                            dve.wait_ge(att_step, s + (st + 2))
                            nc.vector.tensor_tensor(sdiff[:], sink[:, bass.ds(n, 1)], negm[:], ALU.add).then_inc(m_ready, 1)
                        if pos == SCALED + STEP * c:
                            dve.wait_ge(p_exp, n * NCH + (c + 1))
                            nc.vector.tensor_tensor(denom[:], rowsum[:], esink[:], ALU.add).then_inc(att_step, 1)
                            dve.wait_ge(att_step, s + (st + 3))
                            nc.vector.reciprocal(rden[:], denom[:]).then_inc(att_step, 1)
                            dve.wait_ge(att_step, s + (st + 4))
                            for u in range(4):
                                last = nc.vector.tensor_scalar(probs[:, u, 0:nk], probs[:, u, 0:nk], rden[:, u:u + 1], None, ALU.mult)
                            last.then_inc(p_norm, 1)
                        if pos == HEADS + STEP * c:
                            head_out(c)

                for g in range(2):
                    splits(CHUNK0["ca"] + g * ND, n * (2 * ND), hook=lambda i: attention(g * ND + i), taken=0)
                    tile = n * (2 * GT) + g * GT
                    h_out(GROUP0["ca"] + g, n * 2, conv[:, bass.ds(tile + UOFF, GT)])
                head_out(NCH - 1)
                dve.wait_ge(o_evacd, n * NCH + (NCH + 1))

            between(CHUNK0["cb"], 0)
            dve.wait_ge(scaled, H0["cb"])
            with dve.Fori(0, GA // 2) as n:
                for g in range(2):
                    splits(CHUNK0["cb"] + g * ND, n * (2 * ND))
                    tile = n * (2 * GT) + g * GT
                    h_out(GROUP0["cb"] + g, n * 2, ps_z[:])

                    def gate_a():
                        dve.wait_ge(f_ready, n * 2 + (Z0["cb"] + g + 1))
                        for a in range(GT):
                            u = conv[:, bass.ds(tile + (UOFF + a), 1)]
                            last = nc.vector.scalar_tensor_tensor(
                                out=u, in0=u, scalar=vecs[:, bass.ds(tile + (V_BIN + CA0 // P + a), 1)],
                                in1=s_buf[:, a:a + 1], op0=ALU.add, op1=ALU.mult)
                        last.then_inc(u_done, 1)

                    between(CHUNK0["cb"] + (g + 1) * ND, n * (2 * ND), gate_a)

            with dve.Fori(0, GA // 2) as n:
                for g in range(2):
                    splits(CHUNK0["ag"] + g * ND, n * (2 * ND))
                    tile = n * (2 * GT) + g * GT
                    h_out(GROUP0["ag"] + g, n * 2, ps_z[:])
                    o = feat[:, bass.ds(tile, GT)]

                    def gate_o():
                        dve.wait_ge(f_ready, n * 2 + (Z0["ag"] + g + 1))
                        nc.vector.tensor_tensor(o, o, s_buf[:], ALU.mult).then_inc(b_ready, 1)

                    def gated_low():
                        dve.wait_ge(b_hi, n * 2 + (g + 1))
                        low(branch[:, bass.ds(tile, GT), 1], o, branch[:, bass.ds(tile, GT), 0]).then_inc(b_done, 1)

                    between(CHUNK0["ag"] + (g + 1) * ND, n * (2 * ND), gate_o, gated_low)

            with dve.Fori(0, GD // 2) as i:
                taps = [(1 + j * (2 * (ND + NC_) - 1) // (TAPS - 1), j) for j in range(TAPS - 1)]

                def conv_taps(pos):
                    for at, j in taps:
                        if at != pos:
                            continue
                        lag = TAPS - 1 - j
                        for a in range(2):
                            if j == 0:
                                dve.wait_ge(conv_init, i * 2 + (a + 1))
                            else:
                                dve.wait_ge(conv_tap, i * (2 * (TAPS - 1)) + (2 * j + a - 1))
                            y = conv[:, bass.ds(i * 2 + a, 1), lag:T]
                            nc.vector.scalar_tensor_tensor(out=y, in0=conv[:, bass.ds(i * 2 + (a + UOFF), 1), 0:T - lag],
                                                           scalar=vecs[:, bass.ds(i * (2 * TAPS) + (V_CW + a * TAPS + j), 1)],
                                                           in1=y, op0=ALU.mult, op1=ALU.add).then_inc(conv_tap, 1)

                for jj in range(2):
                    base = jj * (ND + NC_)
                    c, g = CHUNK0["attn"] + base, GROUP0["attn"] + 2 * jj
                    cd, gd = i * (2 * (ND + NC_)), i * 4
                    splits(c, cd, hook=lambda k: conv_taps(base + k))
                    h_out(g, gd, ps_z[:])
                    between(c + ND, cd)
                    splits(c + ND, cd, NC_, hook=lambda k: conv_taps(base + ND + k))
                    whole_out(g + 1, gd, s_buf[:])
                    dve.wait_ge(f_ready, i * 2 + (Z0["attn"] + jj + 1))
                    dve.wait_ge(evacd, gd + (g + 2))
                    nc.vector.tensor_tensor(feat[:, bass.ds(i * (2 * GT) + jj * GT, GT)], s_buf[:], g_buf[:], ALU.mult).then_inc(y_done, 1)
                    between(c + ND + NC_, cd)

            def conv_gate(n, g):
                tile = n * (2 * GT) + g * GT
                nc.vector.tensor_tensor(s_buf[:], conv[:, bass.ds(tile, GT)], over_tiles(GT), ALU.mult).then_inc(ln_ready, 1)
                h_out(GROUP0["cg"] + g, n * 2, ps_z[:])

                def gate_conv():
                    dve.wait_ge(ln_act, n * 4 + (2 * g + 2))
                    dve.wait_ge(f_ready, n * 2 + (Z0["cg"] + g + 1))
                    nc.vector.tensor_tensor(g_buf[:], g_buf[:], s_buf[:], ALU.mult).then_inc(b_ready, 1)

                def gated_low():
                    dve.wait_ge(b_hi, n * 2 + (GA + g + 1))
                    low(branch[:, bass.ds(tile, GT), 1], g_buf[:], branch[:, bass.ds(tile, GT), 0]).then_inc(b_done, 1)

                between(CHUNK0["cg"] + (g + 1) * ND, n * (2 * ND), gate_conv, gated_low)

            def centre(pos):
                if pos == 1:
                    dve.wait_ge(stat_done, 2)
                    nc.vector.tensor_scalar(rstd[:], ps_s[:, 0:T], 1.0 / DC, None, ALU.mult).then_inc(ln_mean, 1)
                    dve.wait_ge(ln_mean, 1)
                for b in (2 * pos - 2, 2 * pos - 1) if 1 <= pos < 5 else ():
                    y = conv[:, 2 * b:2 * b + 2]
                    nc.vector.tensor_tensor(y, y, over_tiles(2), ALU.subtract).then_inc(ln_cent, 1)
                if pos == ND - 1:
                    dve.wait_ge(ln_cent, KC // 2)
                    dve.wait_ge(stat_done, 3)
                    norm(1, DC, LN_EPS)

            splits(CHUNK0["cg"], hook=centre)
            conv_gate(0, 0)
            splits(CHUNK0["cg"] + ND)
            conv_gate(0, 1)
            with dve.Fori(1, GA // 2) as n:
                for g in range(2):
                    splits(CHUNK0["cg"] + g * ND, n * (2 * ND))
                    conv_gate(n, g)

            def y_low(i):
                if i >= ND:
                    return
                dve.wait_ge(y_hi, i + 1)
                r = slice(CK * i, CK * i + CK)
                low(mov[:, r, 1], feat[:, r], mov[:, r, 0]).then_inc(mov_ready, 1)

            def conv_out(j, late=None):
                c, g, gd = CHUNK0["conv"], GROUP0["conv"], j * 2
                splits(c, j * (ND + NC_))
                h_out(g, gd, ps_z[:])
                between(c + ND, j * (ND + NC_))
                splits(c + ND, j * (ND + NC_), NC_, hook=late)
                whole_out(g + 1, gd, s_buf[:])
                dve.wait_ge(f_ready, j + (Z0["conv"] + 1))
                dve.wait_ge(evacd, gd + (g + 2))
                nc.vector.tensor_tensor(s_buf[:], s_buf[:], g_buf[:], ALU.mult).then_inc(y_done, 1)
                dve.wait_ge(y_done, j * 2 + (GD + 1))
                y = feat[:, bass.ds(j * GT, GT)]
                nc.vector.tensor_tensor(y, y, s_buf[:], ALU.add).then_inc(y_done, 1)
                between(c + ND + NC_, j * (ND + NC_))

            with dve.Fori(0, GD - 1) as j:
                conv_out(j)
            conv_out(GD - 1, y_low)

            splits(CHUNK0["out"], first=lambda i: y_low(i + Y_EARLY))
            whole_out(GROUP0["out"], 0, feat[:, 0:GT])
            between(CHUNK0["out"] + ND, 0)
            splits(CHUNK0["out"] + ND)
            whole_out(GROUP0["out"] + 1, 0, feat[:, GT:2 * GT])
            between(CHUNK0["out"] + 2 * ND, 0)
            dve.wait_ge(p_hi, 1)
            low(p_mov[:, :, 1], p_raw[:], p_mov[:, :, 0]).then_inc(p_ready, 1)
            with dve.Fori(1, GD // 2) as n:
                for g in range(2):
                    splits(CHUNK0["out"] + g * ND, n * (2 * ND))
                    whole_out(GROUP0["out"] + g, n * 2, feat[:, bass.ds(n * (2 * GT) + g * GT, GT)])
                    between(CHUNK0["out"] + (g + 1) * ND, n * (2 * ND))

            def x1_scale(i):
                if 0 <= i < ND:
                    dve.wait_ge(yg_ready, CK * (i + 1))
                    y = feat[:, CK * i:CK * i + CK]
                    nc.vector.tensor_tensor(y, y, over_tiles(CK), ALU.mult).then_inc(x1_part, 1)

            def x1_low(i):
                if 0 <= i < ND:
                    dve.wait_ge(x1_hi, i + 1)
                    r = slice(CK * i, CK * i + CK)
                    low(mov[:, r, 1], feat[:, r], mov[:, r, 0]).then_inc(mov_ready, 1)

            def x1(pos):
                if pos == X1_FIRST:
                    dve.wait_ge(stat_done, 4)
                    norm(2, D, RMS_EPS)
                    x1_scale(0)
                    x1_scale(1)
                elif pos > X1_FIRST:
                    x1_scale(pos - X1_FIRST + 1)
                    x1_low(pos - X1_FIRST - 1)

            for i in range(GD // 2):
                x1(i)
                if i >= TAKEN:
                    split_at(CHUNK0["ple"] + i)

            def gate_group(g, j):
                whole_out(GROUP0["gate"] + g, j, ps_z[:])
                split_at(CHUNK0["gate"] + (g + 1) * ND, j * ND)
                dve.wait_ge(f_ready, j + (Z0["gate"] + g + 1))
                e = e_ft[:, bass.ds(j * GT + g * GT, GT)]
                nc.vector.tensor_tensor(e, e, s_buf[:], ALU.mult).then_inc(e_ready, 1)
                split_at(CHUNK0["gate"] + (g + 1) * ND + 1, j * ND)

            splits(CHUNK0["gate"], first=lambda i: x1(GD // 2 + i), taken=0)
            gate_group(0, 0)
            splits(CHUNK0["gate"] + ND)
            gate_group(1, 0)
            with dve.Fori(1, GD // 2 - 1) as n:
                for g in range(2):
                    splits(CHUNK0["gate"] + g * ND, n * (2 * ND))
                    gate_group(g, n * 2)
            for g in range(GD - 2, GD):
                splits(CHUNK0["gate"] + g * ND)
                gate_group(g, 0)

            dve.wait_ge(stat_done, 5)
            norm(3, D, RMS_EPS)
            dve.wait_ge(eg_ready, KT)
            for b in range(ND):
                r = slice(CK * b, CK * b + CK)
                nc.vector.tensor_tensor(e_ft[:, r], e_ft[:, r], over_tiles(CK), ALU.mult).then_inc(o_step, 1)
                if b % 2:
                    dve.wait_ge(o_step, b)
                    r = slice(CK * (b - 1), CK * b)
                    nc.vector.tensor_tensor(e_ft[:, r], e_ft[:, r], feat[:, r], ALU.add).then_inc(o_ready[0], 1)

        @block.tensor
        def _(pe):
            def products(c, dyn, g, operand, kt0, last_kt, i=0):
                slot, s = c % RING, 2 * (g % 2)
                for a in range(GT):
                    for k in range(CK):
                        kt = kt0 + k
                        nc.tensor.matmul(ps[:, s + a, :], w_hi[:, slot, k, a * P:a * P + P], operand[:, kt],
                                         start=(kt == 0), stop=False, skip_group_check=True)
                        last = nc.tensor.matmul(ps[:, s + a, T:], w_lo[:, slot, k, a * P:a * P + P], operand[:, kt, 0],
                                                start=False, stop=(kt == last_kt), skip_group_check=True)
                last.then_inc(w_used, 1)

            def group(c, dyn, g, gdyn, operand, nk=ND, block_ready=None, hook=None):
                if g >= 2 or not isinstance(gdyn, int):
                    pe.wait_ge(evacd, gdyn + (g - 1))
                for i in range(nk):
                    pe.wait_ge(w_lo_ready, dyn + (c + i + 1))
                    if block_ready is not None:
                        pe.wait_ge(mov_ready, block_ready + i + 1)
                    products(c + i, dyn, g, operand, CK * i, CK * nk - 1)
                    if hook:
                        hook(i)

            def total(src, out):
                for a in range(GT):
                    last = nc.tensor.matmul(out, ones_sb[:], src[:, a], start=(a == 0), stop=(a == 1),
                                            skip_group_check=True)
                return last

            for b in range(ND):
                pe.wait_ge(mov_ready, b + 1)
                for g in range(2):
                    if b == ND - 2 and g == 1:
                        pe.wait_ge(ones_landed, 16)
                        pe.wait_ge(sum_added, SUM_X + KT // 2)
                        total(sums, ps_s[:, 0:T]).then_inc(stat_done, 1)
                    pe.wait_ge(w_lo_ready, 2 * b + g + 1)
                    products(2 * b + g, 0, g, mov, CK * b, KT - 1)

            def stage(name, n, hook=None):
                for g in range(2):
                    group(CHUNK0[name] + g * ND, n * (2 * ND), GROUP0[name] + g, n * 2, mov,
                          hook=(lambda i: hook(g * ND + i)) if hook else None)

            with pe.Fori(0, GA // 2) as n:
                stage("q", n)

            pe.wait_ge(kv_ready, 2)
            pe.wait_ge(att_landed, 32)
            for a, dst in enumerate((ps_t, ps_sc)):
                for c in range(NCH):
                    t0, nk = (c - 1) * CHUNK if c else 0, P if c else CHUNK
                    last = nc.tensor.transpose(dst[0:nk, c, :], kv_t[:, GT + a, t0:t0 + nk], ident_sb[:])
            last.then_inc(vt_done, 1)

            with pe.Fori(0, NKV) as n:
                def attention(pos):
                    for c in range(NCH):
                        t0, nk = (c - 1) * CHUNK if c else 0, P if c else CHUNK
                        if pos == TURN + STEP * c:
                            pe.wait_ge(p_norm, n * NCH + (c + 1))
                            for u in range(4):
                                last = nc.tensor.transpose(ps_t[:, u, :], probs[:, u, :], ident_sb[:])
                            last.then_inc(t_done, 1)
                        if pos == VALUES + STEP * c:
                            pe.wait_ge(vt_copied, 3)
                            pe.wait_ge(pt_ready, n * NCH + (c + 1))
                            pe.wait_ge(o_evacd, n * NCH + (c + 1))
                            for h in range(2):
                                last = nc.tensor.matmul(ps_o[HD * h:HD * h + HD, :, 0:CHUNK], v_st[0:nk, c, :],
                                                        probs_t[0:nk, 2 * h:2 * h + 2, :].rearrange("k a (b t) -> k (a b) t", t=CHUNK),
                                                        start=True, stop=True)
                            last.then_inc(pv_done, 1)
                    for c in range(NCH):
                        t0, nk = (c - 1) * CHUNK if c else 0, P if c else CHUNK
                        if pos == SCORES + STEP * c:
                            if c == 0:
                                pe.wait_ge(staged, n + 1)
                            for u in range(4):
                                h, pair = u // 2, u % 2
                                last = nc.tensor.matmul(score[u][:, 0:nk],
                                                        q_st[HD * h:HD * h + HD, c, 2 * pair:2 * pair + 2].rearrange("d a t -> d (a t)"),
                                                        k_st[HD * h:HD * h + HD, t0:t0 + nk], start=True, stop=True)
                            last.then_inc(sc_done, 1)

                stage("ca", n, attention)

            with pe.Fori(0, GA // 2) as n:
                stage("cb", n)
            with pe.Fori(0, GA // 2) as n:
                stage("ag", n)

            with pe.Fori(0, GD) as j:
                group(CHUNK0["attn"], j * (ND + NC_), GROUP0["attn"], j * 2, mov)
                pe.wait_ge(b_done, GA)
                group(CHUNK0["attn"] + ND, j * (ND + NC_), GROUP0["attn"] + 1, j * 2, branch, NC_)

            def layer_norm(i):
                if i == 1:
                    pe.wait_ge(sum_added, SUM_MEAN + KC // 2)
                    total(sums, ps_s[:, 0:T]).then_inc(stat_done, 1)
                if i == ND - 2:
                    pe.wait_ge(sum_added, SUM_LN + KC // 2)
                    total(sums, ps_s[:, 0:T]).then_inc(stat_done, 1)

            group(CHUNK0["cg"], 0, GROUP0["cg"], 0, mov, hook=layer_norm)
            group(CHUNK0["cg"] + ND, 0, GROUP0["cg"] + 1, 0, mov)
            with pe.Fori(1, GA // 2) as n:
                stage("cg", n)

            with pe.Fori(0, GD) as j:
                group(CHUNK0["conv"], j * (ND + NC_), GROUP0["conv"], j * 2, mov)
                pe.wait_ge(b_done, 2 * GA)
                group(CHUNK0["conv"] + ND, j * (ND + NC_), GROUP0["conv"] + 1, j * 2, branch, NC_)

            group(CHUNK0["out"], 0, GROUP0["out"], 0, mov, block_ready=ND)
            group(CHUNK0["out"] + ND, 0, GROUP0["out"] + 1, 0, mov)
            with pe.Fori(1, GD // 2) as n:
                for g in range(2):
                    group(CHUNK0["out"] + g * ND, n * (2 * ND), GROUP0["out"] + g, n * 2, mov)

            pe.wait_ge(p_ready, 1)
            for i in range(GD // 2):
                c = CHUNK0["ple"] + i
                pe.wait_ge(w_lo_ready, c + 1)
                for s in range(2):
                    if i == 0:
                        pe.wait_ge(evacd, GROUP0["ple"] + s - 1)
                    else:
                        pe.wait_ge(ple_out, 2 * i + s - 1)
                    for a in range(GT):
                        for k in range(2):
                            col = (GT * s + a) * P
                            hi, lo = (w[:, c % RING, 2 * k + col // GW, col % GW:col % GW + P] for w in (w_hi, w_lo))
                            acc = ps[:, 2 * s + a, 0:T]
                            nc.tensor.matmul(acc, hi, p_mov[:, k, 0], start=(k == 0), stop=False)
                            nc.tensor.matmul(acc, hi, p_mov[:, k, 1], start=False, stop=False)
                            last = nc.tensor.matmul(acc, lo, p_mov[:, k, 0], start=False, stop=(k == 1))
                    last.then_inc(w_used if s else ple_half, 1)
                if i == X1_FIRST - 1:
                    pe.wait_ge(sum_added, SUM_OUT + GD)
                    total(sums, ps_s[:, 0:T]).then_inc(stat_done, 1)

            pe.wait_ge(ple_out, GD - 1)
            group(CHUNK0["gate"], 0, GROUP0["gate"], 0, mov, block_ready=2 * ND)
            pe.wait_ge(ple_out, GD)
            group(CHUNK0["gate"] + ND, 0, GROUP0["gate"] + 1, 0, mov)
            with pe.Fori(1, GD // 2) as n:
                for g in range(2):
                    group(CHUNK0["gate"] + g * ND, n * (2 * ND), GROUP0["gate"] + g, n * 2, mov)
            pe.wait_ge(sum_added, SUM_E + GD)
            total(sums, ps_s[:, 0:T]).then_inc(stat_done, 1)


def kernel(**inputs):
    import concourse.bacc as bacc
    from concourse.bass_utils import run_bass_kernel_spmd

    def lay(name, shape=None):
        a = np.asarray(inputs[name])[0]
        return np.ascontiguousarray(a if shape is None else a.reshape(shape))

    def columns(name):
        return np.asarray(inputs[name])[0].reshape(-1, P).T

    taps = np.asarray(inputs["conv_w"])[0].reshape(TAPS, KC, P).transpose(2, 1, 0).reshape(P, KC * TAPS)
    vec = np.concatenate([columns(n) for n in ("b_in", "b_merge", "pre_norm_g", "post_norm_g", "ple_norm_g",
                                               "conv_b", "conv_ln_g", "conv_ln_b")] + [taps], axis=1)
    heads = np.asarray(inputs["attn_sinks"])[0].reshape(NKV, 2, 2, 2).transpose(2, 0, 3, 1).reshape(2, NKV * 4)
    arrays = {
        "xT": np.ascontiguousarray(np.asarray(inputs["x"])[0].T),
        "pT": np.ascontiguousarray(np.asarray(inputs["p"])[0, 0].T),
        "vec": np.ascontiguousarray(vec),
        "sinks": np.ascontiguousarray(np.repeat(heads, CHUNK, axis=0)),
        "ident": np.eye(P, dtype=np.float32),
        "ones": np.ones((P, P), np.float32),
        "w_in": lay("w_in"), "w_conv_out": lay("w_conv_out"), "w_attn_out": lay("w_attn_out"),
        "w_merge": lay("w_merge"), "w_out": lay("w_out"), "w_ple": lay("w_ple"), "w_gate": lay("w_ple_gate"),
    }
    nc = bacc.Bacc("TRN2", target_bir_lowering=False, num_devices=1)
    args = [nc.dram_tensor(f"{n}_dram", a.shape, mybir.dt.from_np(a.dtype), kind="ExternalInput").ap() for n, a in arrays.items()]
    out = nc.dram_tensor("outT_dram", (D, T), F32, kind="ExternalOutput").ap()
    build(nc, *args, out)
    r = run_bass_kernel_spmd(nc, [{f"{n}_dram": a for n, a in arrays.items()}], core_ids=[0])
    return np.ascontiguousarray(r.results[0]["outT_dram"].T)[None]
```
